# Optimizing a Trainium2 kernel written in Bass

```python
import jax, jax.numpy as jnp
from jax import lax
import numpy as np

D_MODEL = 1024
BATCH = 1
SEQ = 512
DEPTH = 2
DEC_BATCH = 8
DEC_SEQ = 1
PAST_LEN = 4096
PAGE_SIZE = 128

MIX_WIDTH = D_MODEL
A_WIDTH = MIX_WIDTH // 2
B_WIDTH = MIX_WIDTH - A_WIDTH
HEAD_DIM = 128
A_HEADS = A_WIDTH // HEAD_DIM
B_HEADS = B_WIDTH // HEAD_DIM
CONV_W = 4
CHUNK = 64
ROPE_BASE = 10000.0
EPS = 1e-6
L2_EPS = 1e-6
FF_RAW = -(-8 * D_MODEL // 3)
D_FF = -(-FF_RAW // 256) * 256
IN_SIZES = (3 * A_WIDTH, A_WIDTH, A_HEADS, A_HEADS, B_WIDTH, B_WIDTH, B_WIDTH, B_WIDTH)
IN_WIDTH = sum(IN_SIZES)

kernel_name = "hybrid_gdn_retention_decoder_step"

def _rmsnorm(x, w):
    xf = x.astype(jnp.float32)
    y = xf * lax.rsqrt(jnp.mean(xf * xf, axis=-1, keepdims=True) + EPS)
    return (y * w.astype(jnp.float32)).astype(x.dtype)

def _l2norm(x):
    return x * lax.rsqrt(jnp.sum(x * x, axis=-1, keepdims=True) + L2_EPS)

def _causal_conv(x, buf, w):
    L = x.shape[1]
    xp = jnp.concatenate([buf.astype(x.dtype), x], axis=1)
    out = xp[:, 0:L] * w[0]
    for i in range(1, CONV_W):
        out = out + xp[:, i:i + L] * w[i]
    return out, xp[:, -(CONV_W - 1):]

def _rope(x, pos):
    half = x.shape[-1] // 2
    inv = ROPE_BASE ** (-jnp.arange(half, dtype=jnp.float32) / half)
    ang = pos[:, None] * inv[None, :]
    cos, sin = jnp.cos(ang), jnp.sin(ang)
    x1, x2 = x[..., :half], x[..., half:]
    return jnp.concatenate([x1 * cos - x2 * sin, x1 * sin + x2 * cos], axis=-1)

def _chunk_prep(ts, L):
    C = min(CHUNK, L)
    pad = (-L) % C
    nc = (L + pad) // C
    out = []
    for t in ts:
        widths = [(0, 0)] * t.ndim
        widths[2] = (0, pad)
        t = jnp.pad(t, widths)
        out.append(t.reshape(t.shape[:2] + (nc, C) + t.shape[3:]))
    return out, C

def _decay_matrix(gc, C):
    tril = jnp.arange(C)[:, None] >= jnp.arange(C)[None, :]
    diff = gc[..., :, None] - gc[..., None, :]
    return jnp.where(tril, jnp.exp(jnp.where(tril, diff, 0.0)), 0.0), tril

def _gated_delta_chunked(q, k, v, g, beta, s0):
    B, H, L, DK = q.shape
    q = q * (DK ** -0.5)
    (q, k, v, g, beta), C = _chunk_prep([q, k, v, g, beta], L)
    gc = jnp.cumsum(g, axis=-1)
    decay, tril = _decay_matrix(gc, C)
    strict = jnp.arange(C)[:, None] > jnp.arange(C)[None, :]
    kb = k * beta[..., None]
    vb = v * beta[..., None]
    a_low = jnp.where(strict, jnp.einsum('bhnid,bhnjd->bhnij', kb, k) * decay, 0.0)
    t_mat = a_low + jnp.eye(C, dtype=a_low.dtype)
    u = lax.linalg.triangular_solve(t_mat, vb, left_side=True, lower=True, unit_diagonal=True)
    w = lax.linalg.triangular_solve(t_mat, kb * jnp.exp(gc)[..., None], left_side=True,
                                    lower=True, unit_diagonal=True)
    a_intra = jnp.where(tril, jnp.einsum('bhnid,bhnjd->bhnij', q, k) * decay, 0.0)

    def step(S, inp):
        qi, ki, ui, wi, gi, ai = inp
        v_new = ui - jnp.einsum('bhcd,bhde->bhce', wi, S)
        o = jnp.einsum('bhcd,bhde->bhce', qi * jnp.exp(gi)[..., None], S) + \
            jnp.einsum('bhij,bhje->bhie', ai, v_new)
        g_last = gi[..., -1]
        S = S * jnp.exp(g_last)[..., None, None] + jnp.einsum(
            'bhcd,bhce->bhde', ki * jnp.exp(g_last[..., None] - gi)[..., None], v_new)
        return S, o

    xs = tuple(jnp.moveaxis(t, 2, 0) for t in (q, k, u, w, gc, a_intra))
    s_fin, o = lax.scan(step, s0.astype(jnp.float32), xs)
    o = jnp.moveaxis(o, 0, 2)
    o = o.reshape(B, H, -1, o.shape[-1])[:, :, :L]
    return o, s_fin

def _retention_chunked(q, k, v, lg, s0):
    B, H, L, DK = q.shape
    k = k * (DK ** -0.5)
    (q, k, v, lg), C = _chunk_prep([q, k, v, lg], L)
    gc = jnp.cumsum(lg, axis=-1)
    decay, tril = _decay_matrix(gc, C)
    a_intra = jnp.einsum('bhnid,bhnjd->bhnij', q, k) * decay

    def step(S, inp):
        qi, ki, vi, gi, ai = inp
        o = jnp.einsum('bhcd,bhde->bhce', qi * jnp.exp(gi)[..., None], S) + \
            jnp.einsum('bhij,bhje->bhie', ai, vi)
        g_last = gi[..., -1]
        S = S * jnp.exp(g_last)[..., None, None] + jnp.einsum(
            'bhcd,bhce->bhde', ki * jnp.exp(g_last[..., None] - gi)[..., None], vi)
        return S, o

    xs = tuple(jnp.moveaxis(t, 2, 0) for t in (q, k, v, gc, a_intra))
    s_fin, o = lax.scan(step, s0.astype(jnp.float32), xs)
    o = jnp.moveaxis(o, 0, 2)
    o = o.reshape(B, H, -1, o.shape[-1])[:, :, :L]
    return o, s_fin

def _heads(t, n):
    B, L, _ = t.shape
    return t.reshape(B, L, n, HEAD_DIM).transpose(0, 2, 1, 3).astype(jnp.float32)

def _head_gated_norm(o, w, gate):
    B, H, L, D = o.shape
    o = o.transpose(0, 2, 1, 3)
    o = o * lax.rsqrt(jnp.mean(o * o, axis=-1, keepdims=True) + EPS) * w.astype(jnp.float32)
    return o.reshape(B, L, H * D) * jax.nn.silu(gate.astype(jnp.float32))

def _mixer(hn, pos, conv_buf, s_gdn, s_ret, w_in, conv_w, a_log, dt_bias, gdn_norm_w,
           ret_norm_w, w_out):
    B, L, _ = hn.shape
    p = hn @ w_in
    idx = [int(i) for i in np.cumsum(IN_SIZES)[:-1]]
    p_qkv, p_z, p_beta, p_alpha, p_bq, p_bk, p_bv, p_bg = jnp.split(p, idx, axis=-1)
    qkv, conv_new = _causal_conv(p_qkv, conv_buf, conv_w)
    qkv = jax.nn.silu(qkv)
    qa, ka, va = jnp.split(qkv, 3, axis=-1)
    qa = _l2norm(_heads(qa, A_HEADS))
    ka = _l2norm(_heads(ka, A_HEADS))
    va = _heads(va, A_HEADS)
    beta = jax.nn.sigmoid(p_beta.astype(jnp.float32)).transpose(0, 2, 1)
    g = (-jnp.exp(a_log.astype(jnp.float32)) * jax.nn.softplus(
        p_alpha.astype(jnp.float32) + dt_bias.astype(jnp.float32))).transpose(0, 2, 1)
    o_a, s_gdn_new = _gated_delta_chunked(qa, ka, va, g, beta, s_gdn)
    o_a = _head_gated_norm(o_a, gdn_norm_w, p_z)
    qb = _rope(_heads(p_bq, B_HEADS), pos)
    kb = _rope(_heads(p_bk, B_HEADS), pos)
    vb = _heads(p_bv, B_HEADS)
    log_gamma = jnp.log1p(-jnp.exp2(-5.0 - jnp.arange(B_HEADS, dtype=jnp.float32)))
    lg = jnp.broadcast_to(log_gamma[None, :, None], (B, B_HEADS, L))
    o_b, s_ret_new = _retention_chunked(qb, kb, vb, lg, s_ret)
    o_b = _head_gated_norm(o_b, ret_norm_w, p_bg)
    cat = jnp.concatenate([o_a, o_b], axis=-1).astype(hn.dtype)
    return cat @ w_out, conv_new, s_gdn_new, s_ret_new

def _swiglu(hn, w_gate_up, w_down):
    gu = hn @ w_gate_up
    gate, up = jnp.split(gu, 2, axis=-1)
    return (jax.nn.silu(gate) * up) @ w_down

def _trunk(x, pos, conv_st, gdn_st, ret_st, w_in, conv_w, a_log, dt_bias, gdn_norm_w,
           ret_norm_w, w_out, norm_mix_pre, norm_mix_post, norm_ffn_pre, norm_ffn_post,
           w_gate_up, w_down):
    h = x
    convs, gdns, rets = [], [], []
    for l in range(DEPTH):
        m, c_new, sg_new, sr_new = _mixer(
            _rmsnorm(h, norm_mix_pre[l]), pos, conv_st[l], gdn_st[l], ret_st[l], w_in[l],
            conv_w[l], a_log[l], dt_bias[l], gdn_norm_w[l], ret_norm_w[l], w_out[l])
        h = h + _rmsnorm(m, norm_mix_post[l])
        f = _swiglu(_rmsnorm(h, norm_ffn_pre[l]), w_gate_up[l], w_down[l])
        h = h + _rmsnorm(f, norm_ffn_post[l])
        convs.append(c_new.astype(conv_st.dtype))
        gdns.append(sg_new.astype(gdn_st.dtype))
        rets.append(sr_new.astype(ret_st.dtype))
    return h, jnp.stack(convs), jnp.stack(gdns), jnp.stack(rets)

def setup_inputs(seed: int = 0) -> dict:
    key = jax.random.key(seed)
    ks = jax.random.split(key, 20)
    f32 = jnp.float32
    nrm = lambda k, s, sc: jax.random.normal(k, s, f32) * sc
    return {
        "x_prompt": nrm(ks[0], (BATCH, SEQ, D_MODEL), 1.0),
        "x_sample": nrm(ks[1], (DEC_BATCH, DEC_SEQ, D_MODEL), 1.0),
        "state_conv": nrm(ks[2], (DEPTH, DEC_BATCH, CONV_W - 1, 3 * A_WIDTH), 1.0),
        "state_gdn": nrm(ks[3], (DEPTH, DEC_BATCH, A_HEADS, HEAD_DIM, HEAD_DIM), 0.5),
        "state_ret": nrm(ks[4], (DEPTH, DEC_BATCH, B_HEADS, HEAD_DIM, HEAD_DIM), 1.0),
        "w_in": nrm(ks[5], (DEPTH, D_MODEL, IN_WIDTH), D_MODEL ** -0.5),
        "conv_w": nrm(ks[6], (DEPTH, CONV_W, 3 * A_WIDTH), CONV_W ** -0.5),
        "a_log": jnp.log(jax.random.uniform(ks[7], (DEPTH, A_HEADS), f32, 1.0, 16.0)),
        "dt_bias": nrm(ks[8], (DEPTH, A_HEADS), 0.1),
        "gdn_norm_w": 1.0 + nrm(ks[9], (DEPTH, HEAD_DIM), 0.02),
        "ret_norm_w": 1.0 + nrm(ks[10], (DEPTH, HEAD_DIM), 0.02),
        "w_out": nrm(ks[11], (DEPTH, MIX_WIDTH, D_MODEL), MIX_WIDTH ** -0.5),
        "norm_mix_pre": 1.0 + nrm(ks[12], (DEPTH, D_MODEL), 0.02),
        "norm_mix_post": 1.0 + nrm(ks[13], (DEPTH, D_MODEL), 0.02),
        "norm_ffn_pre": 1.0 + nrm(ks[14], (DEPTH, D_MODEL), 0.02),
        "norm_ffn_post": 1.0 + nrm(ks[15], (DEPTH, D_MODEL), 0.02),
        "w_gate_up": nrm(ks[16], (DEPTH, D_MODEL, 2 * D_FF), D_MODEL ** -0.5),
        "w_down": nrm(ks[17], (DEPTH, D_FF, D_MODEL), D_FF ** -0.5),
    }

def reference(x_prompt, x_sample, state_conv, state_gdn, state_ret, w_in, conv_w, a_log,
              dt_bias, gdn_norm_w, ret_norm_w, w_out, norm_mix_pre, norm_mix_post,
              norm_ffn_pre, norm_ffn_post, w_gate_up, w_down):
    weights = (w_in, conv_w, a_log, dt_bias, gdn_norm_w, ret_norm_w, w_out, norm_mix_pre,
               norm_mix_post, norm_ffn_pre, norm_ffn_post, w_gate_up, w_down)
    bp, lp = x_prompt.shape[0], x_prompt.shape[1]
    pos_p = jnp.arange(lp, dtype=jnp.float32)
    conv0 = jnp.zeros((DEPTH, bp, CONV_W - 1, 3 * A_WIDTH), x_prompt.dtype)
    gdn0 = jnp.zeros((DEPTH, bp, A_HEADS, HEAD_DIM, HEAD_DIM), x_prompt.dtype)
    ret0 = jnp.zeros((DEPTH, bp, B_HEADS, HEAD_DIM, HEAD_DIM), x_prompt.dtype)
    y_prompt, conv_p, gdn_p, ret_p = _trunk(x_prompt, pos_p, conv0, gdn0, ret0, *weights)
    ls = x_sample.shape[1]
    pos_s = PAST_LEN + jnp.arange(ls, dtype=jnp.float32)
    y_sample, conv_s, gdn_s, ret_s = _trunk(x_sample, pos_s, state_conv, state_gdn, state_ret,
                                            *weights)
    return (y_prompt, y_sample, conv_p, gdn_p, ret_p, conv_s, gdn_s, ret_s)


_drawn_inputs = setup_inputs


def setup_inputs(seed=0):
    import zlib

    import numpy as np

    out = dict(_drawn_inputs(seed))
    spreads = {}
    factors = {}
    for name, (base, spread) in spreads.items():
        noise = np.random.default_rng([zlib.crc32(name.encode()), seed]).standard_normal(out[name].shape)
        drawn = base * np.exp(spread * noise) if base else spread * noise
        out[name] = __import__('jax').numpy.asarray(drawn.astype(out[name].dtype))
    for name, factor in factors.items():
        out[name] = (out[name] * factor).astype(out[name].dtype)
    return out
```

```python
import math

import concourse.bass as bass
import numpy as np
from concourse import mybir
from contextlib import ExitStack


def trunk(nc, x_prompt, x_sample, state_conv, state_gdn, state_ret, w_in, conv_w, a_log, dt_bias,
          gdn_norm_w, ret_norm_w, w_out, norm_mix_pre, norm_mix_post, norm_ffn_pre, norm_ffn_post,
          w_gate_up, w_down, c_f32, c_rope, c_mask, y_prompt, y_sample, conv_prompt, gdn_prompt,
          ret_prompt, conv_sample, gdn_sample, ret_sample):
    fp32 = mybir.dt.float32
    fp32r = mybir.dt.float32r
    bf16 = mybir.dt.bfloat16
    ALU = mybir.AluOpType
    ACT = mybir.ActivationFunctionType

    P = 128
    DEPTH, D, IN_W = w_in.shape
    KT = D // P
    SEQ = x_prompt.shape[1]
    NB = x_sample.shape[0]
    HALF = SEQ // 2
    NBH = NB // 2
    HC = HALF + NBH
    NC = SEQ // P
    H = state_gdn.shape[2]
    CW = conv_w.shape[1]
    QKV = 3 * H
    FT = w_down.shape[1] // P
    EPS = 1e-6
    L2_EPS = 1e-6
    LEVELS = int(math.log2(P))
    ACT_STEPS = 73
    DVE_STEPS = 265

    IN_T = 8 * H
    OUT_T = KT
    GU_T = 2 * FT
    PIECES = [6, 6, 5, 5]
    assert sum(PIECES) == FT
    DN_S = KT * len(PIECES)
    SLABS = IN_T + OUT_T + GU_T + DN_S
    TILES = IN_T + OUT_T + GU_T + KT
    S_OUT, S_GU, S_DN = IN_T, IN_T + OUT_T, IN_T + OUT_T + GU_T
    T_OUT, T_GU, T_DN = IN_T, IN_T + OUT_T, IN_T + OUT_T + GU_T
    NS = 2
    NW = 2

    C_ID, C_ONE, C_LE, C_GT, C_GQ, C_GV, C_GC, C_GS = 0, P, 2 * P, 3 * P, 4 * P, 4 * P + H, 4 * P + 2 * H, 4 * P + 3 * H
    NCF = 4 * P + 4 * H
    R_MPRE, R_MPOST, R_FPRE, R_FPOST = 0, KT, 2 * KT, 3 * KT
    R_CONV = 4 * KT
    R_GN = R_CONV + CW * QKV
    R_RN = R_GN + 1
    NR = R_RN + 1
    RAW = CW - 1 + SEQ + CW * NB
    CONV_N = RAW - (CW - 1)

    ctx = ExitStack()
    with ctx:
        def sb(name, shape, dt=fp32):
            return ctx.enter_context(nc.sbuf_tensor(name, shape, dt))

        def sem(name):
            return ctx.enter_context(nc.semaphore(name))

        hT = sb("hT", [P, KT, 2, HC])
        cf = sb("cf", [P, NCF])
        mask = sb("mask", [P, LEVELS, P], bf16)
        rope = sb("rope", [P, 2, 2, HC])
        stage = sb("stage", [P, NS, KT, P])
        Wh = sb("Wh", [P, NW, KT, P], fp32r)
        Wl = sb("Wl", [P, NW, KT, P], fp32r)
        wba = sb("wba", [P, KT, 2 * H])
        wbah = sb("wbah", [P, KT, 2 * H], fp32r)
        wbal = sb("wbal", [P, KT, 2 * H], fp32r)
        rb = sb("rb", [P, 2, HC])
        ss = sb("ss", [P, 2, HC])
        sqb = sb("sqb", [P, 2, 2, HC])
        upd = sb("upd", [P, 2, HC])
        prows = sb("prows", [NR, P])
        prm = sb("prm", [P, NR])
        adt = sb("adt", [P, 2, H])
        xdec = sb("xdec", [P, KT, NB])
        NG = NC + NB
        rm = sb("rm", [P, NG])
        ga = sb("ga", [P, NG, 2 * H])
        gb = sb("gb", [P, NG, H])
        gs = sb("gs", [P, NG, H])
        beta = sb("beta", [P, NG, H])
        g = sb("g", [P, NG, H])
        badec = sb("badec", [NB, 2 * H])
        bad = sb("bad", [NB, NB, 2 * H])
        lrq = sb("lrq", [P, NC, 2 * H])
        rq = sb("rq", [P, NC, 2 * H])
        egc = sb("egc", [P, 2, NC, H])
        c2 = sb("c2", [P, NC, H])
        rqs = sb("rqs", [P, NC, H])
        rqs2 = sb("rqs2", [P, NC, H])
        gq2 = sb("gq2", [P, H])
        brk = sb("brk", [P, NC, H])
        c1 = sb("c1", [P, NC, H])
        qkvD = sb("qkvD", [P, QKV, NB])
        rD = sb("rD", [P, 3 * H, NB])
        histT = sb("histT", [P, QKV, NB, CW - 1])
        tailT = sb("tailT", [P, QKV, CW - 1 + NB])
        oD = sb("oD", [P, 2 * H, NB])
        sqd = sb("sqd", [P, 2 * H, NB])
        rqd = sb("rqd", [P, 2 * H, NB])
        arkd = sb("arkd", [P, H, NB])
        brkd = sb("brkd", [P, H, NB])
        du = sb("du", [P, NB])
        dn = sb("dn", [P, 2 * H, NB])
        drm = sb("drm", [P, 2 * H, NB])
        adec = sb("adec", [P, NB, H])
        catD = sb("catD", [P, 2 * H, NB])
        nrm = sb("nrm", [P, 4, H])

        base = nc.sbuf_base
        AR = 27712
        X_F = KT * 2 * HC
        fence = sb("fence", [P, 2 * X_F + AR])
        XH0, XL0, A0 = base, base + 4 * X_F, base + 8 * X_F

        def at(name, where, off, shape, dt=fp32):
            return nc.alloc_sbuf_tensor_at(name, shape, dt, offset=where + 4 * off)

        Xh = at("Xh", XH0, 0, [P, KT, 2, HC], fp32r)
        Xl = at("Xl", XL0, 0, [P, KT, 2, HC], fp32r)
        U = H * P
        Xinv = at("Xinv", XH0, 0, [P, NC, H, P])
        crow = at("crow", XH0, NC * U, [CW - 1 + NB, QKV * P])
        MT = at("MT", XL0, 0, [P, NC, H, P])
        dstate = at("dstate", XL0, NC * U, [P, 2, NB, P])
        sqk = at("sqk", XL0, 0, [P, 2 * H, SEQ])
        fT = at("fT", XL0, 0, [P, KT, 2, HC])

        o = 0
        qkvT = at("qkvT", A0, o, [P, QKV, SEQ])
        mT = at("mT", A0, o, [P, KT, 2, HC])
        PT = at("PT", A0, o + 2 * H * SEQ, [P, NC, H, P])
        o += QKV * SEQ
        rT = at("rT", A0, o, [P, 3 * H, SEQ])
        o += 3 * H * SEQ
        gates = at("gates", A0, o, [P, 2 * H, 2, HC])
        o += 2 * H * 2 * HC
        XT = at("XT", A0, o, [P, NC, H, P])
        raw = at("raw", A0, o, [P, 2, RAW])
        o += NC * U
        ktok = at("ktok", A0, o, [P, NC, H, P])
        conv = at("conv", A0, o, [P, 2, CONV_N])
        o += NC * U
        bv = at("bv", A0, o, [P, NC, H, P])
        rsw = at("rsw", A0, o, [P, 2, 2, HC])
        o += NC * U
        T = at("T", A0, o, [P, 8, H, P])
        hist = at("hist", A0, o, [NB * (CW - 1), QKV * P])
        rcs = at("rcs", A0, o + QKV * P, [P, 2, 2, HC])
        vblk = at("vblk", A0, o, [NB, NB, P])
        krow = at("krow", A0, o + NB * P, [NB, 2, P])
        dtmp = at("dtmp", A0, o + NB * P + 2 * P, [P, NB, P])
        o += 8 * U
        S = at("S", A0, o, [P, H, P])
        o += U
        Sr = at("Sr", A0, o, [P, H, P])
        o += U
        assert o == AR, o
        assert 2 * RAW + 2 * CONV_N <= 2 * NC * U and 2 * RAW <= NC * U + NC * U
        actH = at("actH", A0, 0, [P, FT, 2, HC], fp32r)
        actL = at("actL", A0, FT * 2 * HC, [P, FT, 2, HC], fp32r)
        gp = at("gp", A0, 2 * FT * 2 * HC, [P, 2, 2, HC])
        up = at("up", A0, 2 * FT * 2 * HC + 4 * HC, [P, 2, HC])
        ab = at("ab", A0, 2 * FT * 2 * HC + 6 * HC, [P, 2, 2, HC])
        xt = at("xt", A0, 0, [P, NC, D])
        xd = at("xd", A0, NC * D, [NB, D])
        ytok = at("ytok", A0, 0, [P, NC, D])
        yd = at("yd", A0, NC * D, [NB, D])
        hd = at("hd", A0, NC * D + D, [P, KT, NB])

        PS = ctx.enter_context(nc.psum_tensor("PS", [P, 8, 512], fp32))

        def bank(i, n=512, rows=P):
            return PS[0:rows, i, 0:n]

        def bank4(i):
            return PS[:, i, :].rearrange("p (h n) -> p h n", h=H)

        def pj(slot):
            return PS[:, 2 * slot:2 * slot + 2, 0:HC]

        ident = cf[:, C_ID:C_ID + P]
        ones = cf[:, C_ONE:C_ONE + P]
        m_le = cf[:, C_LE:C_LE + P]
        m_gt = cf[:, C_GT:C_GT + P]

        def over_heads(m):
            return m.unsqueeze(1).to_broadcast([P, H, P])

        def over_cols(v, n=P):
            return v.unsqueeze(2).to_broadcast([P, v.shape[1], n])

        names = (
            "const_loaded x_loaded param_loaded wba_loaded hist_loaded rope_loaded slab0_loaded slab1_loaded "
            "dstate0_loaded dstate1_loaded conv_stored state_stored dstate0_stored dstate1_stored y_stored "
            "slab_done x_T param_T hist_T norm_sum ba_done bad_done tail_T stat_done v_T chunk_mm decay_mm "
            "y_mm x_mm ks_mm vn_mm od_mm out_T rtr_mm rod_mm dks_mm dk_T dv_T dout_mm do_mm dsum_mm y_T "
            "tile_free x_moved hist_ready h_ready x_ready sq_free xdec_ready gate_pre "
            "badiag_ready conv_done crow_ready decay_in bv_ready chunk_used inv_init "
            "y_ready x_new s_ready r_ready vs_ready o_ready osum_ready on_ready catf_ready cat_ready "
            "rv_ready rs_ready dv_ready dblk_ready dstate_new do_moved dsq_ready dcat_ready "
            "a_ready act_ready hd_ready y_moved g_ready "
            "sq_ready rb_ready xh_ready silu_done gates_done gate_exp sqk_ready stat_exp ktok_ready dk_ready "
            "osq_ready orms_ready cath_ready rk_ready gate_silu ah_ready drms_ready dcath_ready "
            "hi_split slab_split wba_hi wba_split mtk_ready "
            "pool_passed pe_passed dve_passed "
            "dve_step act_step").split()
        s = {n: sem(n) for n in names}

        def alone(eng):
            eng.sem_inc(s[{nc.gpsimd: "pool_passed", nc.tensor: "pe_passed", nc.vector: "dve_passed"}[eng]], 1)

        class Steps:

            def __init__(self, eng, own):
                self.eng, self.own, self.base, self.n, self.outer = eng, own, 0, 0, []

            def __call__(self, ins):
                self.n += 1
                ins.then_inc(self.own, 1)
                self.eng.wait_ge(self.own, self.base + self.n)

            def enter(self, i, per):
                self.outer.append((self.base, self.n, per))
                self.base, self.n = self.base + self.n + i * per, 0

            def leave(self, count):
                base, n, per = self.outer.pop()
                assert self.n == per, (self.n, per)
                self.base, self.n = base, n + count * per

        def split_of(l, n):
            return l * SLABS + n + 1 + NS

        def done_of(l, n):
            return l * SLABS + n + 1 + NW

        def one(ap):
            r = ap.shape
            return ap.rearrange("p o a -> p (o a)") if len(r) == 3 else ap.rearrange("p o a b -> p (o a) b")

        def tile_of(t, k):
            return t[:, bass.ds(k, 1)].rearrange("p o a n -> p (o a) n")

        def halves(ap):
            return ap.rearrange("p (a n) -> p a n", a=2)

        block = ctx.enter_context(nc.Block())

        @block.sync
        def _(sp):
            sp.sem_inc(s["state_stored"], 1)
            sp.dma_start(cf[:], c_f32).then_inc(s["const_loaded"], 16)
            sp.dma_start(mask[:], c_mask).then_inc(s["const_loaded"], 16)
            sp.dma_start(xt[:], x_prompt[0].rearrange("(c p) d -> p c d", p=P)).then_inc(s["x_loaded"], 16)
            sp.dma_start(xd[:], x_sample.rearrange("b o d -> (b o) d")).then_inc(s["x_loaded"], 16)
            with sp.Fori(0, DEPTH) as l:
                def slab(n, slot, cols, rows=(0, KT), w=w_in):
                    sp.wait_ge(s["slab_split"], split_of(l, n) - NS)
                    k0, k1 = rows
                    src = w[bass.ds(l, 1), k0 * P:k1 * P, cols].rearrange("o (k p) n -> p (o k) n", p=P)
                    sp.dma_start(stage[:, slot, 0:k1 - k0, :], src).then_inc(s[f"slab{slot}_loaded"], 16)

                sp.wait_ge(s["param_T"], l + 1)
                for w, r in ((norm_mix_pre, R_MPRE), (norm_mix_post, R_MPOST), (norm_ffn_pre, R_FPRE), (norm_ffn_post, R_FPOST)):
                    sp.dma_start(prows[r:r + KT, :], w[bass.ds(l, 1), :].rearrange("o (k n) -> (o k) n", n=P)).then_inc(s["param_loaded"], 16)
                sp.dma_start(prows[R_CONV:R_GN, :], conv_w[bass.ds(l, 1), :, :].rearrange("o w (t n) -> (o w t) n", n=P)).then_inc(s["param_loaded"], 16)
                sp.dma_start(prows[R_GN:R_GN + 1, :], gdn_norm_w[bass.ds(l, 1), :]).then_inc(s["param_loaded"], 16)
                sp.dma_start(prows[R_RN:R_RN + 1, :], ret_norm_w[bass.ds(l, 1), :]).then_inc(s["param_loaded"], 16)
                sp.wait_ge(s["slab_done"], done_of(l, -1))
                for i, w in enumerate((dt_bias, a_log)):
                    sp.dma_start(adt[:, i, :], w[bass.ds(l, 1), :].to_broadcast([P, H])).then_inc(s["param_loaded"], 16)
                sp.dma_start(wba[:], w_in[bass.ds(l, 1), :, 4 * H * P:4 * H * P + 2 * H].rearrange("o (k p) n -> p (o k) n", p=P)).then_inc(s["wba_loaded"], 16)
                sp.dma_start(hist[:], state_conv[bass.ds(l, 1)].rearrange("o b i n -> (o b i) n")).then_inc(s["hist_loaded"], 16)
                sp.dma_start(rope[:], c_rope).then_inc(s["rope_loaded"], 16)
                sp.dma_start(conv_sample[bass.ds(l, 1), :, 0:CW - 2, :].rearrange("o b i n -> (o b) i n"), state_conv[bass.ds(l, 1), :, 1:CW - 1, :].rearrange("o b i n -> (o b) i n")).then_inc(s["conv_stored"], 16)
                with sp.Fori(0, 4 * H // NS) as i:
                    for u in range(NS):
                        slab(i * NS + u, u, bass.ds((i * NS + u) * P, P))
                with sp.Fori(0, 4 * H // NS) as i:
                    for u in range(NS):
                        slab(i * NS + (u + 4 * H), u, bass.ds((i * NS + u) * P + (4 * H * P + 2 * H), P))
                sp.wait_ge(s["crow_ready"], l + 1)
                sp.dma_start(conv_prompt[bass.ds(l, 1), 0, :, :].rearrange("o i n -> (o i) n"), crow[0:CW - 1, :]).then_inc(s["conv_stored"], 16)
                sp.dma_start(conv_sample[bass.ds(l, 1), :, CW - 2, :].rearrange("o b n -> (o b) n"), crow[CW - 1:CW - 1 + NB, :]).then_inc(s["conv_stored"], 16)
                for w in range(2 * H + 2):
                    if w >= 2:
                        st = gdn_sample if w - 2 < H else ret_sample
                        h = (w - 2) % H
                        sp.wait_ge(s["dstate_new"], l * 2 * H + (w - 1))
                        sp.dma_start(st[bass.ds(l, 1), :, h, :, :].rearrange("o b d e -> d (o b) e"), dstate[:, w % 2, :, :]).then_inc(s[f"dstate{w % 2}_stored"], 16)
                    if w < 2 * H:
                        st = state_gdn if w < H else state_ret
                        if w >= 2:
                            sp.wait_ge(s[f"dstate{w % 2}_stored"], (l * H + w // 2) * 16)
                            sp.wait_ge(s["do_mm"], l * 2 * H + (w - 1))
                        else:
                            sp.wait_ge(s["stat_done"], l + 1)
                        sp.dma_start(dstate[:, w % 2, :, :], st[bass.ds(l, 1), :, w % H, :, :].rearrange("o b d e -> d (o b) e")).then_inc(s[f"dstate{w % 2}_loaded"], 16)
                with sp.Fori(0, OUT_T // NS) as i:
                    for u in range(NS):
                        slab(i * NS + (u + S_OUT), u, bass.ds((i * NS + u) * P, P), w=w_out)
                sp.wait_ge(s["s_ready"], (l + 1) * (NC + 1))
                sp.dma_start(gdn_prompt[bass.ds(l, 1), 0].rearrange("o h d e -> d (o h) e"), S[:]).then_inc(s["state_stored"], 16)
                sp.wait_ge(s["rs_ready"], (l + 1) * (NC + 1))
                sp.dma_start(ret_prompt[bass.ds(l, 1), 0].rearrange("o h d e -> d (o h) e"), Sr[:]).then_inc(s["state_stored"], 16)
                with sp.Fori(0, FT) as i:
                    for u in range(2):
                        slab(i * 2 + (u + S_GU), u, bass.ds(i * P + u * FT * P, P), w=w_gate_up)
                with sp.Fori(0, KT) as i:
                    k = 0
                    for u, n in enumerate(PIECES):
                        slab(i * len(PIECES) + (u + S_DN), u % NS, bass.ds(i * P, P), rows=(k, k + n), w=w_down)
                        k += n
            for c in range(NC):
                sp.wait_ge(s["y_moved"], c + 1)
                sp.dma_start(y_prompt[0, c * P:(c + 1) * P, :], ytok[:, c, :]).then_inc(s["y_stored"], 16)
            sp.wait_ge(s["y_moved"], NC + 1)
            sp.dma_start(y_sample.rearrange("b o d -> (b o) d"), yd[:]).then_inc(s["y_stored"], 16)
            sp.wait_ge(s["conv_stored"], DEPTH * 48)
            sp.wait_ge(s["state_stored"], DEPTH * 32 + 1)
            for slot in range(2):
                sp.wait_ge(s[f"dstate{slot}_stored"], DEPTH * H * 16)
            sp.wait_ge(s["y_stored"], 16 * (NC + 1))

        @block.gpsimd
        def _(pool):
            pool.sem_inc(s["slab_split"], NS)
            with pool.Fori(0, DEPTH) as l:
                def split(r, slot, k=KT):
                    n = r * NS + slot
                    pool.wait_ge(s[f"slab{slot}_loaded"], (l * (SLABS // NS) + r + 1) * 16)
                    pool.wait_ge(s["slab_done"], done_of(l, n) - NW)
                    alone(pool)
                    nc.gpsimd.tensor_scalar(Wh[:, slot, 0:k, :], stage[:, slot, 0:k, :], 1.0, 1.0, ALU.mult, ALU.mult).then_inc(s["hi_split"], 1)
                    pool.wait_ge(s["hi_split"], l * SLABS + n + 1)
                    nc.gpsimd.tensor_tensor(Wl[:, slot, 0:k, :], stage[:, slot, 0:k, :], Wh[:, slot, 0:k, :].bitcast(fp32), ALU.subtract).then_inc(s["slab_split"], 1)
                    pool.wait_ge(s["slab_split"], split_of(l, n))

                pool.wait_ge(s["wba_loaded"], l * 16 + 16)
                alone(pool)
                nc.gpsimd.tensor_scalar(wbah[:], wba[:], 1.0, 1.0, ALU.mult, ALU.mult).then_inc(s["wba_hi"], 1)
                pool.wait_ge(s["wba_hi"], l + 1)
                nc.gpsimd.tensor_tensor(wbal[:], wba[:], wbah[:].bitcast(fp32), ALU.subtract).then_inc(s["wba_split"], 1)
                alone(pool)
                with pool.Fori(0, IN_T // NS) as i:
                    for u in range(NS):
                        split(i, u)
                pool.wait_ge(s["inv_init"], l + 1)
                alone(pool)
                with pool.Fori(0, LEVELS) as k:
                    for c in range(NC):
                        n = l * (LEVELS * NC) + k * NC + c
                        pool.wait_ge(s["y_mm"], n + 1)
                        alone(pool)
                        mk = mask[:, bass.ds(k, 1), :].to_broadcast([P, H, P])
                        nc.gpsimd.tensor_tensor(T[:, c % 2], MT[:, c], mk, ALU.mult).then_inc(s["mtk_ready"], 1)
                        pool.wait_ge(s["mtk_ready"], n + 1)
                alone(pool)
                with pool.Fori(0, (OUT_T + GU_T) // NS) as i:
                    for u in range(NS):
                        split(i + S_OUT // NS, u)
                alone(pool)
                with pool.Fori(0, KT) as i:
                    for u, n in enumerate(PIECES):
                        split(i * (len(PIECES) // NS) + (u + S_DN) // NS, u % NS, n)

        @block.tensor
        def _(pe):
            mm, tr = nc.tensor.matmul, nc.tensor.transpose
            pe.sem_inc(s["slab_done"], NW)
            pe.sem_inc(s["y_mm"], 2)
            pe.sem_inc(s["param_T"], 1)
            pe.sem_inc(s["norm_sum"], 1)
            pe.wait_ge(s["const_loaded"], 32)
            pe.wait_ge(s["x_loaded"], 32)
            for k in range(KT):
                if k >= 4:
                    pe.wait_ge(s["x_moved"], k - 3)
                for c in range(NC):
                    last = tr(PS[:, k % 4, c * P:(c + 1) * P], xt[:, c, k * P:(k + 1) * P], ident)
                last.then_inc(s["x_T"], 1)
            for k in range(KT):
                last = tr(PS[:, 4, k * NB:(k + 1) * NB], xd[:, k * P:(k + 1) * P], cf[0:NB, C_ID:C_ID + NB])
            last.then_inc(s["x_T"], 1)
            pe.wait_ge(s["x_moved"], KT + 2)

            with pe.Fori(0, DEPTH) as l:
                def project(n, t, slot, x, k0=0, k=KT, first=True, end=True, ready=None, wslot=None):
                    wslot = slot if wslot is None else wslot
                    pe.wait_ge(s["slab_split"], split_of(l, n))
                    if first:
                        pe.wait_ge(s["tile_free"], l * TILES + t + 1)
                    xh, xl = x
                    for j in range(k):
                        if ready:
                            ready(k0 + j)
                        for w, xx in ((Wh, xh), (Wh, xl), (Wl, xh)):
                            for half in range(2):
                                go = first and j == 0 and w is Wh and xx is xh
                                stop = end and j == k - 1 and w is Wl
                                last = mm(PS[:, 2 * slot + half, 0:HC], w[:, wslot, j, :], xx[:, k0 + j, half, :], start=go, stop=stop)
                    last.then_inc(s["slab_done"], 1)

                def norm_sum(n):
                    pe.wait_ge(s["sq_free"], (l * 4 + n + 1) * KT + 2)
                    for half in range(2):
                        last = mm(PS[:, 4 + half, 0:HC], ones, ss[:, half, :], start=True, stop=True)
                    if n == 0:
                        for c in range(NC):
                            last = mm(PS[:, 6, c:c + 1], ss[:, c // 2, (c % 2) * P:(c % 2 + 1) * P], ones[:, 0:1], start=True, stop=True)
                    last.then_inc(s["norm_sum"], 1)

                pe.wait_ge(s["param_loaded"], (l + 1) * 9 * 16)
                pe.wait_ge(s["rb_ready"], l * 4 + 1)
                tr(PS[:, 4, 0:NR], prows[:], cf[0:NR, C_ID:C_ID + NR]).then_inc(s["param_T"], 1)
                pe.wait_ge(s["hist_loaded"], (l + 1) * 16)
                alone(pe)
                nh = NB * (CW - 1)
                for t in range(QKV):
                    last = tr(PS[:, 5, t * nh:(t + 1) * nh], hist[:, t * P:(t + 1) * P], cf[0:nh, C_ID:C_ID + nh])
                last.then_inc(s["hist_T"], 1)
                pe.wait_ge(s["hist_ready"], l + 1)

                X = (Xh, Xl)
                for u in range(2):
                    project(u, u, u, X, ready=(lambda k: pe.wait_ge(s["x_ready"], l * 2 * KT + k + 1)) if u == 0 else None)
                norm_sum(0)
                pe.wait_ge(s["wba_split"], l + 1)
                for c in range(NC):
                    for j in range(KT):
                        for a, b in ((Xh, wbah), (Xl, wbah), (Xh, wbal)):
                            mm(PS[:, 7, c * 2 * H:(c + 1) * 2 * H], a[:, j, c // 2, (c % 2) * P:(c % 2 + 1) * P], b[:, j, :], start=j == 0 and a is Xh and b is wbah, stop=j == KT - 1 and b is wbal)
                pe.wait_ge(s["xdec_ready"], l + 1)
                for j in range(KT):
                    last = mm(PS[0:NB, 7, 64:64 + 2 * H], xdec[:, j, :], wba[:, j, :], start=j == 0, stop=j == KT - 1)
                last.then_inc(s["ba_done"], 1)
                pe.wait_ge(s["badiag_ready"], l + 1)
                pe.wait_ge(s["rb_ready"], l * 4 + 2)
                mm(PS[:, 6, 64:64 + NB * 2 * H], cf[0:NB, C_ONE:C_ONE + P], bad[:].rearrange("a b n -> a (b n)"), start=True, stop=True).then_inc(s["bad_done"], 1)
                alone(pe)
                with pe.Fori(0, (IN_T - 2) // 2) as i:
                    for u in range(2):
                        n = i * 2 + (u + 2)
                        project(n, n, u, X)

                pe.wait_ge(s["conv_done"], (l + 1) * QKV)
                pe.wait_ge(s["gate_pre"], l + 1)
                nt = CW - 1 + NB
                for t in range(QKV):
                    last = tr(PS[0:nt, 4 + t // 4, (t % 4) * P:(t % 4 + 1) * P], tailT[:, t, :], ident)
                last.then_inc(s["tail_T"], 1)
                pe.wait_ge(s["sqk_ready"], l + 1)
                for c in range(NC):
                    for t in range(2 * H):
                        last = mm(PS[:, 7, c * 2 * H + t:c * 2 * H + t + 1], sqk[:, t, c * P:(c + 1) * P], ones[:, 0:1], start=True, stop=True)
                pe.wait_ge(s["g_ready"], l + 1)
                gp_ = g[:, 0:NC, :].rearrange("p c h -> p (c h)")
                mm(PS[:, 7, 64:64 + NC * H], m_le, gp_, start=True, stop=True)
                mm(PS[:, 7, 80:80 + NC * H], ones, gp_, start=True, stop=True)
                mm(PS[:, 7, 128:128 + 2 * H * NB], ones, sqd[:].rearrange("p a b -> p (a b)"), start=True, stop=True).then_inc(s["stat_done"], 1)

                pe.wait_ge(s["crow_ready"], l + 1)
                pe.wait_ge(s["stat_exp"], l + 1)
                pe.wait_ge(s["tile_free"], l * TILES + IN_T + 2)
                for w in range(2 * H):
                    n = l * 2 * H + w
                    gdn = w < H
                    k_of, q_of = (qkvD[:, H + w, :], qkvD[:, w, :]) if gdn else (rD[:, w, :], rD[:, w - H, :])
                    pe.wait_ge(s[f"dstate{w % 2}_loaded"], (l * H + (w // 2 + 1)) * 16)
                    if gdn:
                        for b in range(NB):
                            last = mm(PS[:, 0, b:b + 1], dstate[:, w % 2, b, :], k_of[:, b:b + 1], start=True, stop=True)
                        last.then_inc(s["dks_mm"], 1)
                    if w:
                        pe.wait_ge(s["dblk_ready"], n)
                    tr(PS[0:NB, 1, 0:P], k_of, ident).then_inc(s["dk_T"], 1)
                    pe.wait_ge(s["dv_ready"], n + 1)
                    tr(PS[0:NB, 2, 0:P], du[:], ident).then_inc(s["dv_T"], 1)
                    pe.wait_ge(s["dblk_ready"], n + 1)
                    if w:
                        pe.wait_ge(s["dstate_new"], n)
                    for half in range(2):
                        last = mm(bank(4 + half), krow[:, 0, :], vblk[:, half * NB // 2:(half + 1) * NB // 2, :].rearrange("a b e -> a (b e)"), start=True, stop=True)
                    last.then_inc(s["dout_mm"], 1)
                    pe.wait_ge(s["dstate_new"], n + 1)
                    if w:
                        pe.wait_ge(s["do_moved"], n)
                    for b in range(NB):
                        last = mm(PS[:, 3, b:b + 1], dstate[:, w % 2, b, :], q_of[:, b:b + 1], start=True, stop=True)
                    last.then_inc(s["do_mm"], 1)
                pe.wait_ge(s["dsq_ready"], l + 1)
                mm(PS[:, 0, 0:2 * H * NB], ones, dn[:].rearrange("p a b -> p (a b)"), start=True, stop=True).then_inc(s["dsum_mm"], 1)

                pe.wait_ge(s["drms_ready"], l + 1)
                for c in range(NC):
                    for h in range(H):
                        last = tr(PS[:, c, h * P:(h + 1) * P], qkvT[:, 2 * H + h, c * P:(c + 1) * P], ident)
                last.then_inc(s["v_T"], 1)
                for c in range(NC):
                    b0 = 4 * (1 - c % 2)
                    if c == 1:
                        pe.wait_ge(s["bv_ready"], l + 1)
                    if c >= 2:
                        pe.wait_ge(s["chunk_used"], l * NC + c - 1)
                        pe.wait_ge(s["ktok_ready"], l * NC + c - 1)
                    cs = slice(c * P, (c + 1) * P)
                    for h in range(H):
                        tr(PS[:, b0, h * P:(h + 1) * P], qkvT[:, H + h, cs], ident)
                    for h in range(H):
                        mm(PS[:, b0 + 1, h * P:(h + 1) * P], qkvT[:, H + h, cs], qkvT[:, H + h, cs], start=True, stop=True)
                    for h in range(H):
                        last = mm(PS[:, b0 + 2, h * P:(h + 1) * P], qkvT[:, H + h, cs], qkvT[:, h, cs], start=True, stop=True)
                    last.then_inc(s["chunk_mm"], 1)
                    pe.wait_ge(s["decay_in"], l * NC + c + 1)
                    for h in range(H):
                        last = mm(PS[:, b0 + 3, h * P:(h + 1) * P], T[:, c % 2, h, :], m_le, start=True, stop=True)
                    last.then_inc(s["decay_mm"], 1)

                pe.wait_ge(s["inv_init"], l + 1)
                pe.wait_ge(s["ktok_ready"], (l + 1) * NC)
                alone(pe)
                with pe.Fori(0, LEVELS) as k:
                    m = l * (LEVELS * NC) + k * NC

                    def left(c):
                        pe.wait_ge(s["x_new"], m + c + 1)
                        pe.wait_ge(s["mtk_ready"], m + c + 1)
                        for h in range(H):
                            last = mm(PS[:, c, h * P:(h + 1) * P], T[:, c % 2, h, :], Xinv[:, c, h, :], start=True, stop=True)
                        last.then_inc(s["y_mm"], 1)

                    def right(c):
                        pe.wait_ge(s["y_ready"], m + c + 1)
                        pe.wait_ge(s["x_new"], m + c + 3)
                        for h in range(H):
                            mm(PS[:, 4 + c % 2, h * P:(h + 1) * P], XT[:, c, h, :], T[:, 2 + c % 2, h, :], start=True, stop=True)
                        for h in range(H):
                            last = mm(PS[:, 6 + c % 2, h * P:(h + 1) * P], T[:, 2 + c % 2, h, :], XT[:, c, h, :], start=True, stop=True)
                        last.then_inc(s["x_mm"], 1)

                    left(0)
                    for c in range(1, NC):
                        left(c)
                        right(c - 1)
                    right(NC - 1)

                def out_rows(n):
                    pe.wait_ge(s["on_ready"], n + 1)
                    for h in range(H):
                        last = tr(PS[:, 5, h * P:(h + 1) * P], T[:, 4, h, :], ident)
                    last.then_inc(s["out_T"], 1)

                pe.wait_ge(s["x_new"], (l + 1) * (LEVELS * NC) + 4)
                for c in range(NC):
                    cs = slice(c * P, (c + 1) * P)
                    pe.wait_ge(s["s_ready"], l * (NC + 1) + c + 1)
                    if c:
                        pe.wait_ge(s["cat_ready"], l * 2 * NC + c)
                    for h in range(H):
                        mm(PS[:, 0, h * P:(h + 1) * P], qkvT[:, H + h, cs], S[:, h, :], start=True, stop=True)
                    for h in range(H):
                        last = mm(PS[:, 1, h * P:(h + 1) * P], qkvT[:, h, cs], S[:, h, :], start=True, stop=True)
                    last.then_inc(s["ks_mm"], 1)
                    pe.wait_ge(s["r_ready"], l * NC + c + 1)
                    for h in range(H):
                        last = mm(PS[:, 2, h * P:(h + 1) * P], XT[:, c, h, :], T[:, 0, h, :], start=True, stop=True)
                    last.then_inc(s["vn_mm"], 1)
                    pe.wait_ge(s["vs_ready"], l * NC + c + 1)
                    for h in range(H):
                        mm(PS[:, 3, h * P:(h + 1) * P], PT[:, c, h, :], T[:, 1, h, :], start=True, stop=True)
                    for h in range(H):
                        last = mm(PS[:, 4, h * P:(h + 1) * P], ktok[:, c, h, :], T[:, 2, h, :], start=True, stop=True)
                    last.then_inc(s["od_mm"], 1)
                    out_rows(l * 2 * NC + c)

                for c in range(NC):
                    cs = slice(c * P, (c + 1) * P)
                    pe.wait_ge(s["cat_ready"], l * 2 * NC + NC + c)
                    pe.wait_ge(s["rs_ready"], l * (NC + 1) + c + 1)
                    for h in range(H):
                        tr(PS[:, 6, h * P:(h + 1) * P], rT[:, H + h, cs], ident)
                    for h in range(H):
                        tr(PS[:, 7, h * P:(h + 1) * P], rT[:, 2 * H + h, cs], ident)
                    for h in range(H):
                        last = mm(PS[:, 0, h * P:(h + 1) * P], rT[:, H + h, cs], rT[:, h, cs], start=True, stop=True)
                    last.then_inc(s["rtr_mm"], 1)
                    pe.wait_ge(s["rk_ready"], l * NC + c + 1)
                    pe.wait_ge(s["rv_ready"], l * NC + c + 1)
                    for h in range(H):
                        mm(PS[:, 1, h * P:(h + 1) * P], rT[:, h, cs], Sr[:, h, :], start=True, stop=False)
                        mm(PS[:, 1, h * P:(h + 1) * P], T[:, 2, h, :], T[:, 1, h, :], start=False, stop=True)
                    for h in range(H):
                        last = mm(PS[:, 2, h * P:(h + 1) * P], T[:, 0, h, :], T[:, 1, h, :], start=True, stop=True)
                    last.then_inc(s["rod_mm"], 1)
                    out_rows(l * 2 * NC + NC + c)

                pe.wait_ge(s["cat_ready"], (l + 1) * 2 * NC)
                pe.wait_ge(s["dcat_ready"], l + 1)
                alone(pe)
                with pe.Fori(0, OUT_T // 2) as i:
                    for u in range(2):
                        n = i * 2 + u
                        project(n + S_OUT, n + T_OUT, u, X)
                norm_sum(1)

                for u in range(2):
                    project(u + S_GU, u + T_GU, u, X, ready=(lambda k: pe.wait_ge(s["x_ready"], l * 2 * KT + KT + k + 1)) if u == 0 else None)
                norm_sum(2)
                alone(pe)
                with pe.Fori(0, FT - 1) as i:
                    for u in range(2):
                        n = i * 2 + (u + 2)
                        project(n + S_GU, n + T_GU, u, X)
                alone(pe)
                with pe.Fori(0, KT // 2) as i:
                    for u in range(2):
                        k0 = 0
                        for q, k in enumerate(PIECES):
                            n = i * 2 * len(PIECES) + (u * len(PIECES) + q)
                            last_piece = q == len(PIECES) - 1
                            if u == 0 and q == 0:
                                pe.wait_ge(s["act_ready"], (l + 1) * FT)
                            project(n + S_DN, i * 2 + (u + T_DN), u, (actH, actL), k0=k0, k=k, first=q == 0, end=last_piece, wslot=q % NW)
                            k0 += k
                norm_sum(3)

            pe.wait_ge(s["h_ready"], KT + DEPTH * 2 * KT)
            pe.wait_ge(s["hd_ready"], 1)
            for c in range(NC):
                if c >= 2:
                    pe.wait_ge(s["y_moved"], c - 1)
                for k in range(KT):
                    last = tr(PS[:, 2 * (c % 2) + k // 4, (k % 4) * P:(k % 4 + 1) * P], hT[:, k, c // 2, (c % 2) * P:(c % 2 + 1) * P], ident)
                last.then_inc(s["y_T"], 1)
            for k in range(KT):
                last = tr(PS[0:NB, 4 + k // 4, (k % 4) * P:(k % 4 + 1) * P], hd[:, k, :], ident)
            last.then_inc(s["y_T"], 1)

        SC = float(P) ** -0.5
        WIN = CW - 1 + SEQ

        @block.scalar
        def _(act):
            A = nc.scalar.activation
            step = Steps(act, s["act_step"])

            def sig(ins, name, count):
                ins.then_inc(s[name], 1)
                act.wait_ge(s[name], count)

            act.sem_inc(s["silu_done"], 2)
            act.sem_inc(s["rb_ready"], 1)
            act.wait_ge(s["const_loaded"], 32)
            with act.Fori(0, DEPTH) as l:
                step.enter(l, ACT_STEPS)

                def square(n, k, src, slot):
                    act.wait_ge(s["sq_free"], (l * 4 + n) * KT + k + 1)
                    sig(A(sqb[:, slot], src, ACT.Square), "sq_ready", (l * 4 + n) * KT + k + 1)

                def rsqrt_mean(n):
                    act.wait_ge(s["norm_sum"], l * 4 + n + 2)
                    if n == 0:
                        step(A(rm[:, 0:NC], PS[:, 6, 0:NC], ACT.Ln, scale=1.0 / D, bias=EPS))
                        step(A(rm[:, 0:NC], rm[:, 0:NC], ACT.Exp, scale=-0.5))
                    step(A(rb[:], PS[:, 4:6, 0:HC], ACT.Ln, scale=1.0 / D, bias=EPS))
                    sig(A(rb[:], rb[:], ACT.Exp, scale=-0.5), "rb_ready", l * 4 + n + 2)

                def prepare(n, row):
                    first = l * 2 * KT + (KT if n else 0)
                    for k in range(KT):
                        act.wait_ge(s["h_ready"], first + k + 1)
                        if n == 0 and k == 0:
                            act.wait_ge(s["hist_ready"], l + 1)
                        sig(A(Xh[:, k], hT[:, k], ACT.Copy, scale=prm[:, row + k:row + k + 1]), "xh_ready", first + k + 1)
                        square(n, k, hT[:, k], k % 2)
                    rsqrt_mean(n)

                prepare(0, R_MPRE)
                with act.Fori(0, QKV // 2) as i:
                    step.enter(i, 2)
                    for u in range(2):
                        n = i * 2 + u
                        act.wait_ge(s["conv_done"], l * QKV + n + 1)
                        step(A(one(qkvT[:, bass.ds(n, 1), :]), conv[:, u, 0:SEQ], ACT.Silu))
                        sig(A(one(qkvD[:, bass.ds(n, 1), :]), conv[:, u, WIN:CONV_N:CW], ACT.Silu), "silu_done", l * QKV + n + 3)
                    step.leave(QKV // 2)
                act.wait_ge(s["tile_free"], l * TILES + IN_T + 2)
                sig(A(gates[:], gates[:], ACT.Silu), "gates_done", l + 1)
                act.wait_ge(s["slab_done"], done_of(l, IN_T - 1))
                step(A(sqk[:], qkvT[:, 0:2 * H, :], ACT.Square))
                sig(A(sqd[:], qkvD[:, 0:2 * H, :], ACT.Square), "sqk_ready", l + 1)
                act.wait_ge(s["gate_pre"], l + 1)
                step(A(gb[:], ga[:, :, 0:H], ACT.Exp, scale=-1.0))
                step(A(adt[:, 1, :], adt[:, 1, :], ACT.Exp))
                step(A(gs[:], gs[:], ACT.Exp, scale=-1.0))
                sig(A(gs[:], gs[:], ACT.Ln, bias=1.0), "gate_exp", l + 1)
                act.wait_ge(s["stat_done"], l + 1)
                step(A(lrq[:].rearrange("p c h -> p (c h)"), PS[:, 7, 0:NC * 2 * H], ACT.Ln, bias=L2_EPS))
                step(A(rqd[:].rearrange("p h b -> p (h b)"), PS[:, 7, 128:128 + 2 * H * NB], ACT.Ln, bias=L2_EPS))
                step(A(rqd[:], rqd[:], ACT.Exp, scale=-0.5))
                step(A(rq[:], lrq[:], ACT.Exp, scale=-0.5))
                step(A(lrq[:], lrq[:], ACT.Copy, scale=-0.5))
                step(A(adec[:], g[:, NC:NG, :], ACT.Exp))
                sig(A(egc[:].rearrange("p a c h -> p (a c h)"), PS[:, 7, 64:64 + 2 * NC * H], ACT.Exp), "stat_exp", l + 1)
                act.wait_ge(s["dsum_mm"], l + 1)
                step(A(drm[:].rearrange("p h b -> p (h b)"), PS[:, 0, 0:2 * H * NB], ACT.Ln, scale=1.0 / P, bias=EPS))
                sig(A(drm[:], drm[:], ACT.Exp, scale=-0.5), "drms_ready", l + 1)
                for c in range(NC):
                    n = l * NC + c
                    act.wait_ge(s["chunk_mm"], n + 1)
                    sig(A(ktok[:, c], bank4(4 * (1 - c % 2)), ACT.Copy), "ktok_ready", n + 1)
                    act.wait_ge(s["decay_mm"], n + 1)
                    if c >= 2:
                        act.wait_ge(s["chunk_used"], n - 1)
                    for h in range(H):
                        ins = A(T[:, 2 + c % 2, h, :], PS[:, 4 * (1 - c % 2) + 3, h * P:(h + 1) * P], ACT.Exp, bias=lrq[:, c, H + h:H + h + 1])
                        if h < H - 1:
                            step(ins)
                        else:
                            sig(ins, "dk_ready", n + 1)

                def finish(n, m, c):
                    act.wait_ge(s["o_ready"], n + 1)
                    for h in range(H):
                        ins = A(T[:, 5, h, :], T[:, 3, h, :], ACT.Square, accum_out=nrm[:, 0, h:h + 1])
                        if h < H - 1:
                            step(ins)
                        else:
                            sig(ins, "osq_ready", n + 1)
                    act.wait_ge(s["osum_ready"], n + 1)
                    step(A(nrm[:, 2, :], nrm[:, 1, :], ACT.Ln, scale=1.0 / P, bias=EPS))
                    sig(A(nrm[:, 2, :], nrm[:, 2, :], ACT.Exp, scale=-0.5), "orms_ready", n + 1)
                    act.wait_ge(s["catf_ready"], n + 1)
                    if m == 0 and c == 0:
                        act.wait_ge(s["conv_stored"], (l + 1) * 48)
                    dst = Xh[:, m * H:(m + 1) * H, c // 2, (c % 2) * P:(c % 2 + 1) * P]
                    sig(A(dst, T[:, 6], ACT.Copy), "cath_ready", n + 1)

                for c in range(NC):
                    finish(l * 2 * NC + c, 0, c)
                for c in range(NC):
                    act.wait_ge(s["rtr_mm"], l * NC + c + 1)
                    sig(A(T[:, 0], bank4(6), ACT.Copy), "rk_ready", l * NC + c + 1)
                    finish(l * 2 * NC + NC + c, 1, c)
                dec = Xh[:].rearrange("p k a n -> p (k a) n")[:, :, HALF:HC]
                sig(A(dec, catD[:].rearrange("p h (a b) -> p (h a) b", a=2), ACT.Copy), "dcath_ready", l + 1)

                def squares_of(n, t0, src):
                    with act.Fori(0, KT // 2) as i:
                        for u in range(2):
                            k = i * 2 + u
                            act.wait_ge(s["tile_free"], l * TILES + k + (t0 + 3))
                            square(n, k, tile_of(src, k), u)
                    rsqrt_mean(n)

                squares_of(1, T_OUT, mT)
                prepare(2, R_FPRE)
                with act.Fori(0, FT // 2) as i:
                    for u in range(2):
                        j = i * 2 + u
                        act.wait_ge(s["tile_free"], l * TILES + j * 2 + (T_GU + 3))
                        sig(A(gp[:, u], gp[:, u], ACT.Silu), "gate_silu", l * FT + j + 1)
                        act.wait_ge(s["a_ready"], l * FT + j + 1)
                        sig(A(tile_of(actH, j), ab[:, u], ACT.Copy), "ah_ready", l * FT + j + 1)
                squares_of(3, T_DN, fT)
                step.leave(DEPTH)

        @block.vector
        def _(dve):
            V = nc.vector
            step = Steps(dve, s["dve_step"])

            def sig(ins, name, count):
                ins.then_inc(s[name], 1)
                dve.wait_ge(s[name], count)

            dve.sem_inc(s["tile_free"], 2)
            dve.sem_inc(s["sq_free"], 2)
            dve.sem_inc(s["x_new"], 4)
            dve.wait_ge(s["const_loaded"], 32)
            for k in range(KT):
                dve.wait_ge(s["x_T"], k + 1)
                sig(V.tensor_copy(hT[:, k, :, 0:HALF], PS[:, k % 4, :].rearrange("p (a n) -> p a n", a=2)), "x_moved", k + 1)
            dve.wait_ge(s["x_T"], KT + 1)
            for a in range(2):
                src = PS[:, 4, 0:KT * NB].rearrange("p (k b) -> p k b", k=KT)[:, :, a * NBH:(a + 1) * NBH]
                sig(V.tensor_copy(hT[:, :, a, HALF:HC], src), "x_moved", KT + 1 + a)
            dve.sem_inc(s["h_ready"], KT)

            with dve.Fori(0, DEPTH) as l:
                step.enter(l, DVE_STEPS)

                def add_squares(n, k, slot, first):
                    dve.wait_ge(s["sq_ready"], (l * 4 + n) * KT + k + 1)
                    if first:
                        dve.wait_ge(s["norm_sum"], l * 4 + n + 1)
                        ins = V.tensor_copy(ss[:], sqb[:, slot])
                    else:
                        ins = V.tensor_tensor(ss[:], ss[:], sqb[:, slot], ALU.add)
                    sig(ins, "sq_free", (l * 4 + n) * KT + k + 3)

                def prepare(n, row):
                    first = l * 2 * KT + (KT if n else 0)
                    for k in range(KT):
                        dve.wait_ge(s["xh_ready"], first + k + 1)
                        sig(V.scalar_tensor_tensor(Xl[:, k], hT[:, k], prm[:, row + k:row + k + 1], Xh[:, k].bitcast(fp32), ALU.mult, ALU.subtract), "x_ready", first + k + 1)
                        add_squares(n, k, k % 2, k == 0)

                def tile_done(t):
                    dve.wait_ge(s["slab_done"], l * SLABS + t + (1 + NW))

                def moved(ins, t):
                    sig(ins, "tile_free", l * TILES + t + 3)

                dve.wait_ge(s["param_T"], l + 2)
                step(V.tensor_copy(prm[:], PS[:, 4, 0:NR]))
                dve.wait_ge(s["hist_T"], l + 1)
                sig(V.tensor_copy(histT[:].rearrange("p t b i -> p (t b i)"), PS[:, 5, 0:QKV * NB * (CW - 1)]), "hist_ready", l + 1)
                wpre = prm[:, R_MPRE:R_MPRE + KT].unsqueeze(2).to_broadcast([P, KT, NBH])
                step(V.tensor_tensor(xdec[:, :, 0:NBH], hT[:, :, 0, HALF:HC], wpre, ALU.mult))
                sig(V.tensor_tensor(xdec[:, :, NBH:NB], hT[:, :, 1, HALF:HC], wpre, ALU.mult), "xdec_ready", l + 1)
                prepare(0, R_MPRE)
                step(V.memset(raw[:, :, 0:CW - 1], 0.0))
                dve.wait_ge(s["state_stored"], l * 32 + 1)
                sig(V.memset(S[:], 0.0), "s_ready", l * (NC + 1) + 1)
                sig(V.memset(Sr[:], 0.0), "rs_ready", l * (NC + 1) + 1)
                dve.wait_ge(s["ba_done"], l + 1)
                step(V.tensor_copy(badec[:], PS[0:NB, 7, 64:64 + 2 * H]))
                eye_rows = cf[0:NB, C_ID:C_ID + NB]
                sig(V.tensor_tensor(bad[:], badec[:].unsqueeze(1).to_broadcast([NB, NB, 2 * H]), eye_rows.unsqueeze(2).to_broadcast([NB, NB, 2 * H]), ALU.mult), "badiag_ready", l + 1)
                dve.wait_ge(s["rb_ready"], l * 4 + 2)
                step(V.tensor_copy(rm[:, NC:NG].rearrange("p (a b) -> p a b", a=2), rb[:, :, HALF:HC]))
                dve.wait_ge(s["rope_loaded"], (l + 1) * 16)
                for r in range(2):
                    step(V.tensor_tensor(rope[:, r], rope[:, r], rb[:], ALU.mult))

                alone(dve)
                with dve.Fori(0, QKV // 2) as i:
                    step.enter(i, 2 * (4 + CW - 1))
                    for u in range(2):
                        t = i * 2 + u
                        tile_done(t)
                        win = raw[:, u, WIN:RAW].rearrange("p (b w) -> p b w", w=CW)
                        step(V.tensor_tensor(raw[:, u, CW - 1:WIN].rearrange("p (a n) -> p a n", a=2), pj(u)[:, :, 0:HALF], rb[:, :, 0:HALF], ALU.mult))
                        moved(V.tensor_tensor(win[:, :, CW - 1].rearrange("p (a b) -> p a b", a=2), pj(u)[:, :, HALF:HC], rb[:, :, HALF:HC], ALU.mult), t)
                        step(V.tensor_copy(win[:, :, 0:CW - 1], one(histT[:, bass.ds(t, 1)])))
                        step(V.tensor_copy(one(tailT[:, bass.ds(t, 1), 0:CW - 1]), raw[:, u, SEQ:WIN]))
                        step(V.tensor_copy(one(tailT[:, bass.ds(t, 1), CW - 1:CW - 1 + NB]), win[:, :, CW - 1]))
                        dve.wait_ge(s["silu_done"], l * QKV + t + 1)
                        wc = [prm[:, bass.ds(t + (R_CONV + w * QKV), 1)] for w in range(CW)]
                        step(V.tensor_scalar(conv[:, u], raw[:, u, 0:CONV_N], wc[0], None, ALU.mult))
                        for w in range(1, CW - 1):
                            step(V.scalar_tensor_tensor(conv[:, u], raw[:, u, w:w + CONV_N], wc[w], conv[:, u], ALU.mult, ALU.add))
                        sig(V.scalar_tensor_tensor(conv[:, u], raw[:, u, CW - 1:RAW], wc[CW - 1], conv[:, u], ALU.mult, ALU.add), "conv_done", l * QKV + t + 1)
                    step.leave(QKV // 2)

                def gate_tiles(t0, g0):
                    alone(dve)
                    with dve.Fori(0, H // 2) as i:
                        for u in range(2):
                            tile_done(i * 2 + (t0 + u))
                            moved(V.tensor_tensor(tile_of(gates, i * 2 + (g0 + u)), pj(u), rb[:], ALU.mult), i * 2 + (t0 + u))

                gate_tiles(QKV, 0)
                h2 = P // 2
                alone(dve)
                with dve.Fori(0, H) as i:
                    step.enter(i, 2 * 4)
                    for u in range(2):
                        j = i * 2 + u
                        t = j + 4 * H
                        tile_done(t)
                        step(V.tensor_tensor(rsw[0:h2, u], PS[h2:P, 2 * u:2 * u + 2, 0:HC], rope[0:h2, 1], ALU.mult))
                        step(V.tensor_tensor(rsw[h2:P, u], PS[0:h2, 2 * u:2 * u + 2, 0:HC], rope[h2:P, 1], ALU.mult))
                        moved(V.tensor_tensor(rcs[:, u], pj(u), rope[:, 0], ALU.mult), t)
                        step(V.tensor_tensor(halves(one(rT[:, bass.ds(j, 1)])), rcs[:, u, :, 0:HALF], rsw[:, u, :, 0:HALF], ALU.add))
                        step(V.tensor_tensor(halves(one(rD[:, bass.ds(j, 1)])), rcs[:, u, :, HALF:HC], rsw[:, u, :, HALF:HC], ALU.add))
                    step.leave(H)
                alone(dve)
                with dve.Fori(0, H // 2) as i:
                    step.enter(i, 2)
                    for u in range(2):
                        j = i * 2 + (u + 2 * H)
                        t = j + 4 * H
                        tile_done(t)
                        step(V.tensor_tensor(halves(one(rT[:, bass.ds(j, 1)])), pj(u)[:, :, 0:HALF], rb[:, :, 0:HALF], ALU.mult))
                        moved(V.tensor_tensor(halves(one(rD[:, bass.ds(j, 1)])), pj(u)[:, :, HALF:HC], rb[:, :, HALF:HC], ALU.mult), t)
                    step.leave(H // 2)
                gate_tiles(7 * H, H)
                dve.wait_ge(s["bad_done"], l + 1)
                dve.wait_ge(s["param_loaded"], (l + 1) * 9 * 16)
                step(V.tensor_tensor(ga[:, 0:NC, :], PS[:, 7, 0:NC * 2 * H].rearrange("p (c h) -> p c h", c=NC), rm[:, 0:NC].unsqueeze(2).to_broadcast([P, NC, 2 * H]), ALU.mult))
                step(V.tensor_tensor(ga[:, NC:NG, :], PS[:, 6, 64:64 + NB * 2 * H].rearrange("p (c h) -> p c h", c=NB), rm[:, NC:NG].unsqueeze(2).to_broadcast([P, NB, 2 * H]), ALU.mult))
                step(V.tensor_tensor(ga[:, :, H:2 * H], ga[:, :, H:2 * H], adt[:, 0, :].unsqueeze(1).to_broadcast([P, NG, H]), ALU.add))
                sig(V.scalar_tensor_tensor(gs[:], ga[:, :, H:2 * H], -1.0, ga[:, :, H:2 * H], ALU.mult, ALU.max), "gate_pre", l + 1)
                dve.wait_ge(s["tail_T"], l + 1)
                sig(V.tensor_copy(crow[:], PS[0:CW - 1 + NB, 4:4 + QKV // 4, :].rearrange("p a n -> p (a n)")), "crow_ready", l + 1)
                dve.wait_ge(s["gate_exp"], l + 1)
                step(V.tensor_scalar(gb[:], gb[:], 1.0, None, ALU.add))
                step(V.reciprocal(beta[:], gb[:]))
                step(V.scalar_tensor_tensor(gs[:], ga[:, :, H:2 * H], 0.0, gs[:], ALU.max, ALU.add))
                sig(V.scalar_tensor_tensor(g[:], gs[:], -1.0, adt[:, 1, :].unsqueeze(1).to_broadcast([P, NG, H]), ALU.mult, ALU.mult), "g_ready", l + 1)
                dve.wait_ge(s["stat_exp"], l + 1)
                step(V.tensor_tensor(brk[:], beta[:, 0:NC, :], rq[:, :, H:2 * H], ALU.mult))
                step(V.tensor_tensor(c1[:], brk[:], egc[:, 0], ALU.mult))
                step(V.tensor_scalar(rqs[:], rq[:, :, 0:H], SC, None, ALU.mult))
                step(V.tensor_tensor(rqs2[:], rqs[:], rqs[:], ALU.mult))
                step(V.tensor_tensor(gq2[:], cf[:, C_GQ:C_GQ + H], cf[:, C_GQ:C_GQ + H], ALU.mult))
                step(V.tensor_tensor(arkd[:], adec[:].rearrange("p b h -> p h b"), rqd[:, H:2 * H, :], ALU.mult))
                step(V.tensor_tensor(brkd[:], beta[:, NC:NG, :].rearrange("p b h -> p h b"), rqd[:, H:2 * H, :], ALU.mult))

                for w in range(2 * H):
                    n = l * 2 * H + w
                    gdn, h = w < H, w % H
                    if gdn:
                        dve.wait_ge(s["dks_mm"], l * H + w + 1)
                        step(V.tensor_tensor(du[:], PS[:, 0, 0:NB], arkd[:, h], ALU.mult))
                        step(V.tensor_tensor(du[:], qkvD[:, 2 * H + h], du[:], ALU.subtract))
                        sig(V.tensor_tensor(du[:], du[:], brkd[:, h], ALU.mult), "dv_ready", n + 1)
                    else:
                        sig(V.tensor_scalar(du[:], rD[:, 2 * H + h], SC, None, ALU.mult), "dv_ready", n + 1)
                    dve.wait_ge(s["dk_T"], n + 1)
                    dve.wait_ge(s["dv_T"], n + 1)
                    for a in range(2):
                        step(V.tensor_copy(krow[:, a], PS[0:NB, 1 + a, 0:P]))
                    sig(V.tensor_tensor(vblk[:], krow[:, 1].unsqueeze(1).to_broadcast([NB, NB, P]), eye_rows.unsqueeze(2).to_broadcast([NB, NB, P]), ALU.mult), "dblk_ready", n + 1)
                    dve.wait_ge(s["dout_mm"], n + 1)
                    dve.wait_ge(s[f"dstate{w % 2}_loaded"], (l * H + (w // 2 + 1)) * 16)
                    outer = PS[:, 4:6, :].rearrange("p a (b e) -> p (a b) e", e=P)
                    if gdn:
                        step(V.tensor_tensor(dtmp[:], dstate[:, w % 2], over_cols(adec[:, :, h]), ALU.mult))
                        sig(V.tensor_tensor(dstate[:, w % 2], dtmp[:], outer, ALU.add), "dstate_new", n + 1)
                    else:
                        sig(V.scalar_tensor_tensor(dstate[:, w % 2], dstate[:, w % 2], cf[:, C_GS + h:C_GS + h + 1], outer, ALU.mult, ALU.add), "dstate_new", n + 1)
                    dve.wait_ge(s["do_mm"], n + 1)
                    if gdn:
                        sig(V.scalar_tensor_tensor(oD[:, w], PS[:, 3, 0:NB], SC, rqd[:, h], ALU.mult, ALU.mult), "do_moved", n + 1)
                    else:
                        sig(V.tensor_copy(oD[:, w], PS[:, 3, 0:NB]), "do_moved", n + 1)
                sig(V.tensor_tensor(dn[:], oD[:], oD[:], ALU.mult), "dsq_ready", l + 1)
                dve.wait_ge(s["drms_ready"], l + 1)
                dve.wait_ge(s["gates_done"], l + 1)
                step(V.tensor_tensor(oD[:], oD[:], drm[:], ALU.mult))
                for m, r in enumerate((R_GN, R_RN)):
                    hs = slice(m * H, (m + 1) * H)
                    step(V.scalar_tensor_tensor(catD[:, hs].rearrange("p h (a b) -> p (h a) b", a=2), oD[:, hs].rearrange("p h (a b) -> p (h a) b", a=2), prm[:, r:r + 1],
                                                gates[:, hs].rearrange("p h a n -> p (h a) n")[:, :, HALF:HC], ALU.mult, ALU.mult))

                dve.wait_ge(s["v_T"], l + 1)
                for c in range(NC):
                    ins = V.tensor_tensor(bv[:, c], bank4(c), over_cols(beta[:, c, :]), ALU.mult)
                    if c < NC - 1:
                        step(ins)
                    else:
                        sig(ins, "bv_ready", l + 1)
                for c in range(NC):
                    n = l * NC + c
                    if c >= 2:
                        dve.wait_ge(s["decay_mm"], n - 1)
                    sig(V.tensor_tensor(T[:, c % 2], over_heads(m_gt), over_cols(g[:, c, :]), ALU.mult), "decay_in", n + 1)
                    dve.wait_ge(s["dk_ready"], n + 1)
                    step(V.tensor_tensor(T[:, 4], T[:, 2 + c % 2], over_heads(m_le), ALU.mult))
                    step(V.tensor_copy(c2[:, c, :], T[:, 4, :, P - 1]))
                    dve.wait_ge(s["chunk_mm"], n + 1)
                    b0 = 4 * (1 - c % 2)
                    step(V.tensor_tensor(MT[:, c], bank4(b0 + 1), T[:, 4], ALU.mult))
                    sig(V.tensor_tensor(PT[:, c], bank4(b0 + 2), T[:, 4], ALU.mult), "chunk_used", n + 1)
                eye = ident.unsqueeze(1).to_broadcast([P, NC * H, P])
                step(V.tensor_copy(Xinv[:].rearrange("p c h n -> p (c h) n"), eye))
                sig(V.tensor_copy(XT[:].rearrange("p c h n -> p (c h) n"), eye), "inv_init", l + 1)

                alone(dve)
                with dve.Fori(0, LEVELS) as k:
                    step.enter(k, NC)
                    m = l * (LEVELS * NC) + k * NC

                    def left(c):
                        dve.wait_ge(s["y_mm"], m + c + 3)
                        sig(V.tensor_tensor(T[:, 2 + c % 2], bank4(c), over_cols(brk[:, c, :]), ALU.mult), "y_ready", m + c + 1)

                    def right(c):
                        dve.wait_ge(s["x_mm"], m + c + 1)
                        step(V.tensor_tensor(Xinv[:, c], Xinv[:, c], bank4(4 + c % 2), ALU.subtract))
                        sig(V.tensor_tensor(XT[:, c], XT[:, c], bank4(6 + c % 2), ALU.subtract), "x_new", m + c + 5)

                    left(0)
                    for c in range(1, NC):
                        left(c)
                        right(c - 1)
                    right(NC - 1)
                    step.leave(LEVELS)

                def finish(n, m, c, a2, a1):
                    dve.wait_ge(s["osq_ready"], n + 1)
                    sig(V.tensor_tensor(nrm[:, 1, :], nrm[:, 0, :], a2, ALU.mult), "osum_ready", n + 1)
                    dve.wait_ge(s["orms_ready"], n + 1)
                    step(V.tensor_tensor(nrm[:, 3, :], nrm[:, 2, :], a1, ALU.mult))
                    sig(V.tensor_tensor(T[:, 4], T[:, 3], over_cols(nrm[:, 3, :]), ALU.mult), "on_ready", n + 1)
                    dve.wait_ge(s["out_T"], n + 1)
                    cols = (slice(None), slice(m * H, (m + 1) * H), c // 2, slice((c % 2) * P, (c % 2 + 1) * P))
                    row = (R_GN, R_RN)[m]
                    sig(V.scalar_tensor_tensor(T[:, 6], bank4(5), prm[:, row:row + 1], gates[cols], ALU.mult, ALU.mult), "catf_ready", n + 1)
                    dve.wait_ge(s["cath_ready"], n + 1)
                    sig(V.tensor_tensor(Xl[cols], T[:, 6], Xh[cols].bitcast(fp32), ALU.subtract), "cat_ready", n + 1)

                for slot in range(2):
                    dve.wait_ge(s[f"dstate{slot}_stored"], (l + 1) * H * 16)
                for c in range(NC):
                    n = l * NC + c
                    dve.wait_ge(s["ks_mm"], n + 1)
                    step(V.tensor_tensor(T[:, 0], bank4(0), over_cols(c1[:, c, :]), ALU.mult))
                    sig(V.tensor_tensor(T[:, 0], bv[:, c], T[:, 0], ALU.subtract), "r_ready", n + 1)
                    step(V.tensor_tensor(T[:, 3], bank4(1), over_cols(egc[:, 0, c, :]), ALU.mult))
                    step(V.tensor_tensor(T[:, 7], S[:], over_cols(egc[:, 1, c, :]), ALU.mult))
                    dve.wait_ge(s["vn_mm"], n + 1)
                    step(V.tensor_copy(T[:, 1], bank4(2)))
                    sig(V.tensor_tensor(T[:, 2], T[:, 1], over_cols(c2[:, c, :]), ALU.mult), "vs_ready", n + 1)
                    dve.wait_ge(s["od_mm"], n + 1)
                    sig(V.tensor_tensor(T[:, 3], T[:, 3], bank4(3), ALU.add), "o_ready", l * 2 * NC + c + 1)
                    sig(V.tensor_tensor(S[:], T[:, 7], bank4(4), ALU.add), "s_ready", l * (NC + 1) + c + 2)
                    finish(l * 2 * NC + c, 0, c, rqs2[:, c, :], rqs[:, c, :])
                for c in range(NC):
                    n = l * NC + c
                    dve.wait_ge(s["rtr_mm"], n + 1)
                    step(V.tensor_tensor(T[:, 1], bank4(7), over_cols(cf[:, C_GV:C_GV + H]), ALU.mult))
                    sig(V.tensor_tensor(T[:, 2], bank4(0), over_heads(m_le), ALU.mult), "rv_ready", n + 1)
                    dve.wait_ge(s["rod_mm"], n + 1)
                    sig(V.tensor_copy(T[:, 3], bank4(1)), "o_ready", l * 2 * NC + NC + c + 1)
                    step(V.tensor_tensor(T[:, 7], Sr[:], bank4(2), ALU.add))
                    sig(V.tensor_tensor(Sr[:], T[:, 7], over_cols(cf[:, C_GC:C_GC + H]), ALU.mult), "rs_ready", l * (NC + 1) + c + 2)
                    finish(l * 2 * NC + NC + c, 1, c, gq2[:], cf[:, C_GQ:C_GQ + H])
                dve.wait_ge(s["dcath_ready"], l + 1)
                dec = Xl[:].rearrange("p k a n -> p (k a) n")[:, :, HALF:HC]
                dech = Xh[:].rearrange("p k a n -> p (k a) n")[:, :, HALF:HC].bitcast(fp32)
                sig(V.tensor_tensor(dec, catD[:].rearrange("p h (a b) -> p (h a) b", a=2), dech, ALU.subtract), "dcat_ready", l + 1)

                def branch(n, t0, s0, per, dst, row, h0):
                    dve.wait_ge(s["norm_sum"], l * 4 + n + 1)
                    step(V.memset(ss[:], 0.0))
                    alone(dve)
                    with dve.Fori(0, KT // 2) as i:
                        for u in range(2):
                            k = i * 2 + u
                            dve.wait_ge(s["slab_done"], l * SLABS + k * per + (s0 + per + NW))
                            moved(V.tensor_copy(tile_of(dst, k), pj(u)), k + t0)
                            add_squares(n, k, u, False)
                    dve.wait_ge(s["rb_ready"], l * 4 + n + 2)
                    for k in range(KT):
                        step(V.scalar_tensor_tensor(upd[:], dst[:, k], prm[:, row + k:row + k + 1], rb[:], ALU.mult, ALU.mult))
                        sig(V.tensor_tensor(hT[:, k], hT[:, k], upd[:], ALU.add), "h_ready", h0 + k + 1)

                branch(1, T_OUT, S_OUT, 1, mT, R_MPOST, l * 2 * KT + KT)
                prepare(2, R_FPRE)
                dve.wait_ge(s["rb_ready"], l * 4 + 4)
                alone(dve)
                with dve.Fori(0, FT // 2) as i:
                    for u in range(2):
                        j = i * 2 + u
                        dve.wait_ge(s["slab_done"], l * SLABS + j * 2 + (S_GU + 1 + NW))
                        moved(V.tensor_tensor(gp[:, u], pj(0), rb[:], ALU.mult), j * 2 + T_GU)
                        dve.wait_ge(s["slab_done"], l * SLABS + j * 2 + (S_GU + 2 + NW))
                        moved(V.tensor_tensor(up[:], pj(1), rb[:], ALU.mult), j * 2 + (T_GU + 1))
                        dve.wait_ge(s["gate_silu"], l * FT + j + 1)
                        sig(V.tensor_tensor(ab[:, u], gp[:, u], up[:], ALU.mult), "a_ready", l * FT + j + 1)
                        dve.wait_ge(s["ah_ready"], l * FT + j + 1)
                        sig(V.tensor_tensor(tile_of(actL, j), ab[:, u], tile_of(actH, j).bitcast(fp32), ALU.subtract), "act_ready", l * FT + j + 1)
                branch(3, T_DN, S_DN, len(PIECES), fT, R_FPOST, l * 2 * KT + 2 * KT)
                step.leave(DEPTH)

            step(V.tensor_copy(hd[:, :, 0:NBH], hT[:, :, 0, HALF:HC]))
            sig(V.tensor_copy(hd[:, :, NBH:NB], hT[:, :, 1, HALF:HC]), "hd_ready", 1)
            for c in range(NC):
                dve.wait_ge(s["y_T"], c + 1)
                b = 2 * (c % 2)
                sig(V.tensor_copy(ytok[:, c, :].rearrange("p (a n) -> p a n", a=2), PS[:, b:b + 2, :]), "y_moved", c + 1)
            dve.wait_ge(s["y_T"], NC + 1)
            sig(V.tensor_copy(yd[:].rearrange("p (a n) -> p a n", a=2), PS[0:NB, 4:6, :]), "y_moved", NC + 1)


_INS = ["x_prompt", "x_sample", "state_conv", "state_gdn", "state_ret", "w_in", "conv_w", "a_log", "dt_bias",
        "gdn_norm_w", "ret_norm_w", "w_out", "norm_mix_pre", "norm_mix_post", "norm_ffn_pre", "norm_ffn_post",
        "w_gate_up", "w_down"]


def _constants(seq, nb, heads, past_len=4096, rope_base=10000.0):
    P = 128
    i = np.arange(P)
    gamma = 1.0 - 2.0 ** (-5.0 - np.arange(heads))
    cols = [np.eye(P), np.ones((P, P)), (i[:, None] <= i[None, :]), (i[:, None] > i[None, :]),
            gamma[None, :] ** (i[:, None] + 1.0), gamma[None, :] ** -(i[:, None] + 1.0) * P ** -0.5,
            np.broadcast_to(gamma[None, :] ** P, (P, heads)), np.broadcast_to(gamma[None, :], (P, heads))]
    c_f32 = np.concatenate([np.asarray(c, np.float64) for c in cols], 1).astype(np.float32)
    half = P // 2
    inv = np.float32(rope_base) ** (-np.arange(half, dtype=np.float32) / np.float32(half))
    at = np.arange(seq, dtype=np.float32)
    new = np.full(nb // 2, past_len, np.float32)
    pos = np.concatenate([at[:seq // 2], new, at[seq // 2:], new])
    ang = (pos[None, :] * inv[:, None]).astype(np.float32).astype(np.float64)
    cos, sin = np.cos(ang), np.sin(ang)
    rope = np.stack([np.concatenate([cos, cos]), np.concatenate([-sin, sin])], 1).astype(np.float32)
    rope = rope.reshape(P, 2, 2, -1)
    mask = np.zeros((P, 7, P))
    for k in range(7):
        j, r = i[:, None], i[None, :]
        mask[:, k, :] = (j >> (k + 1) == r >> (k + 1)) & ((r >> k) & 1 == 1) & ((j >> k) & 1 == 0)
    return c_f32, rope, mask


def kernel(**inputs):
    import concourse.bacc as bacc
    import ml_dtypes
    from concourse.bass_utils import run_bass_kernel_spmd

    nc = bacc.Bacc("TRN2", target_bir_lowering=False, num_devices=1)
    arrays, args = {}, []

    def add(name, a):
        arrays[name] = a
        args.append(nc.dram_tensor(name, a.shape, mybir.dt.from_np(a.dtype), kind="ExternalInput").ap())

    for name in _INS:
        add(f"in_{name}", np.ascontiguousarray(inputs[name]))
    depth, nb, heads, dim, _ = inputs["state_gdn"].shape
    _, seq, d = inputs["x_prompt"].shape
    cw = inputs["conv_w"].shape[1]
    c_f32, rope, mask = _constants(seq, nb, heads)
    add("c_f32", c_f32)
    add("c_rope", rope)
    add("c_mask", mask.astype(ml_dtypes.bfloat16))
    width = 3 * heads * dim
    outs = [(1, seq, d), (nb, 1, d), (depth, 1, cw - 1, width), (depth, 1, heads, dim, dim),
            (depth, 1, heads, dim, dim), (depth, nb, cw - 1, width), (depth, nb, heads, dim, dim),
            (depth, nb, heads, dim, dim)]
    for i, shape in enumerate(outs):
        args.append(nc.dram_tensor(f"out_{i}", shape, mybir.dt.float32, kind="ExternalOutput").ap())
    trunk(nc, *args)
    r = run_bass_kernel_spmd(nc, [arrays], core_ids=[0])
    return tuple(r.results[0][f"out_{i}"] for i in range(len(outs)))
```

```python
import math

import concourse.bass as bass
import numpy as np
from concourse import mybir
from contextlib import ExitStack


def trunk(nc, x_prompt, x_sample, state_conv, state_gdn, state_ret, w_in, conv_w, a_log, dt_bias,
          gdn_norm_w, ret_norm_w, w_out, norm_mix_pre, norm_mix_post, norm_ffn_pre, norm_ffn_post,
          w_gate_up, w_down, c_f32, c_rope, c_mask, y_prompt, y_sample, conv_prompt, gdn_prompt,
          ret_prompt, conv_sample, gdn_sample, ret_sample):
    fp32 = mybir.dt.float32
    fp32r = mybir.dt.float32r
    bf16 = mybir.dt.bfloat16
    ALU = mybir.AluOpType
    ACT = mybir.ActivationFunctionType

    P = 128
    DEPTH, D, IN_W = w_in.shape
    KT = D // P
    SEQ = x_prompt.shape[1]
    NB = x_sample.shape[0]
    HALF = SEQ // 2
    NBH = NB // 2
    HC = HALF + NBH
    NC = SEQ // P
    H = state_gdn.shape[2]
    CW = conv_w.shape[1]
    QKV = 3 * H
    FT = w_down.shape[1] // P
    EPS = 1e-6
    L2_EPS = 1e-6
    LEVELS = int(math.log2(P))
    ACT_STEPS = 78
    DVE_STEPS = 242

    IN_T = 8 * H
    OUT_T = KT
    GU_T = 2 * FT
    PIECES = [6, 6, 5, 5]
    assert sum(PIECES) == FT
    DN_S = KT * len(PIECES)
    SLABS = IN_T + OUT_T + GU_T + DN_S
    TILES = IN_T + OUT_T + GU_T + KT
    S_OUT, S_GU, S_DN = IN_T, IN_T + OUT_T, IN_T + OUT_T + GU_T
    T_OUT, T_GU, T_DN = IN_T, IN_T + OUT_T, IN_T + OUT_T + GU_T
    NS = 2
    NW = 2

    C_ID, C_ONE, C_LE, C_GT, C_GQ, C_GV, C_GC, C_GS = 0, P, 2 * P, 3 * P, 4 * P, 4 * P + H, 4 * P + 2 * H, 4 * P + 3 * H
    NCF = 4 * P + 4 * H
    R_MPRE, R_MPOST, R_FPRE, R_FPOST = 0, KT, 2 * KT, 3 * KT
    R_CONV = 4 * KT
    R_GN = R_CONV + CW * QKV
    R_RN = R_GN + 1
    NR = R_RN + 1
    RAW = CW - 1 + SEQ + CW * NB
    CONV_N = RAW - (CW - 1)

    ctx = ExitStack()
    with ctx:
        def sb(name, shape, dt=fp32):
            return ctx.enter_context(nc.sbuf_tensor(name, shape, dt))

        def sem(name):
            return ctx.enter_context(nc.semaphore(name))

        hT = sb("hT", [P, KT, 2, HC])
        cf = sb("cf", [P, NCF])
        mask = sb("mask", [P, LEVELS, P], bf16)
        rope = sb("rope", [P, 2, 2, HC])
        stage = sb("stage", [P, NS, KT, P])
        Wh = sb("Wh", [P, NW, KT, P], fp32r)
        Wl = sb("Wl", [P, NW, KT, P], fp32r)
        wba = sb("wba", [P, KT, 2 * H])
        rb = sb("rb", [P, 2, HC])
        ss = sb("ss", [P, 2, HC])
        sqb = sb("sqb", [P, 2, 2, HC])
        upd = sb("upd", [P, 2, HC])
        prows = sb("prows", [NR, P])
        prm = sb("prm", [P, NR])
        adt = sb("adt", [P, 2, H])
        NG = NC + NB
        ga = sb("ga", [P, NG, 2 * H])
        gb = sb("gb", [P, NG, H])
        gs = sb("gs", [P, NG, H])
        beta = sb("beta", [P, NG, H])
        g = sb("g", [P, NG, H])
        bad = sb("bad", [2 * H, NB, 2 * H])
        lrq = sb("lrq", [P, NC, 2 * H])
        rq = sb("rq", [P, NC, 2 * H])
        egc = sb("egc", [P, 2, NC, H])
        c2 = sb("c2", [P, NC, H])
        rqs = sb("rqs", [P, NC, H])
        rqs2 = sb("rqs2", [P, NC, H])
        gq2 = sb("gq2", [P, H])
        brk = sb("brk", [P, NC, H])
        c1 = sb("c1", [P, NC, H])
        qkvD = sb("qkvD", [P, QKV, NB])
        rD = sb("rD", [P, 3 * H, NB])
        histT = sb("histT", [P, QKV, NB, CW - 1])
        tailT = sb("tailT", [P, QKV, CW - 1 + NB])
        oD = sb("oD", [P, 2 * H, NB])
        sqd = sb("sqd", [P, 2 * H, NB])
        rqd = sb("rqd", [P, 2 * H, NB])
        arkd = sb("arkd", [P, H, NB])
        brkd = sb("brkd", [P, H, NB])
        du = sb("du", [P, NB])
        dn = sb("dn", [P, 2 * H, NB])
        drm = sb("drm", [P, 2 * H, NB])
        adec = sb("adec", [P, NB, H])
        catD = sb("catD", [P, 2 * H, NB])
        nrm = sb("nrm", [P, 4, H])

        base = nc.sbuf_base
        AR = 27712
        X_F = KT * 2 * HC
        fence = sb("fence", [P, 2 * X_F + AR])
        XH0, XL0, A0 = base, base + 4 * X_F, base + 8 * X_F

        def at(name, where, off, shape, dt=fp32):
            return nc.alloc_sbuf_tensor_at(name, shape, dt, offset=where + 4 * off)

        Xh = at("Xh", XH0, 0, [P, KT, 2, HC], fp32r)
        Xl = at("Xl", XL0, 0, [P, KT, 2, HC], fp32r)
        U = H * P
        Xinv = at("Xinv", XH0, 0, [P, NC, H, P])
        crow = at("crow", XH0, NC * U, [CW - 1 + NB, QKV * P])
        MT = at("MT", XL0, 0, [P, NC, H, P])
        dstate = at("dstate", XL0, H * 2 * HC, [P, 2, NB, P])
        fT = at("fT", XL0, 0, [P, KT, 2, HC])

        o = 0
        qkvT = at("qkvT", A0, o, [P, QKV, SEQ])
        mT = at("mT", A0, o, [P, KT, 2, HC])
        PT = at("PT", A0, o + 2 * H * SEQ, [P, NC, H, P])
        o += QKV * SEQ
        rT = at("rT", A0, o, [P, 3 * H, SEQ])
        o += 3 * H * SEQ
        gates = at("gates", A0, o, [P, 2 * H, 2, HC])
        o += 2 * H * 2 * HC
        XT = at("XT", A0, o, [P, NC, H, P])
        raw = at("raw", A0, o, [P, 2, RAW])
        o += NC * U
        ktok = at("ktok", A0, o, [P, NC, H, P])
        conv = at("conv", A0, o, [P, 2, CONV_N])
        o += NC * U
        bv = at("bv", A0, o, [P, NC, H, P])
        rcs = at("rcs", A0, o - NC * U + 2 * CONV_N, [P, 2, 2, HC])
        rsw = at("rsw", A0, o - NC * U + 2 * CONV_N + 4 * HC, [P, 2, 2, HC])
        o += NC * U
        T = at("T", A0, o, [P, 8, H, P])
        hist = at("hist", A0, o, [NB * (CW - 1), QKV * P])
        sqk = at("sqk", A0, o, [P, 2 * H, SEQ])
        o += 8 * U
        S = at("S", A0, o, [P, H, P])
        o += U
        Sr = at("Sr", A0, o, [P, H, P])
        o += U
        assert o == AR, o
        assert 2 * CONV_N + 8 * HC <= 2 * NC * U
        assert 2 * RAW + 2 * CONV_N <= 2 * NC * U and 2 * RAW <= NC * U + NC * U
        actH = at("actH", A0, 0, [P, FT, 2, HC], fp32r)
        actL = at("actL", A0, FT * 2 * HC, [P, FT, 2, HC], fp32r)
        gp = at("gp", A0, 2 * FT * 2 * HC, [P, 2, 2, HC])
        up = at("up", A0, 2 * FT * 2 * HC + 4 * HC, [P, 2, HC])
        ab = at("ab", A0, 2 * FT * 2 * HC + 6 * HC, [P, 2, 2, HC])
        xt = at("xt", A0, 0, [P, NC, D])
        xd = at("xd", A0, NC * D, [NB, D])
        ytok = at("ytok", A0, 0, [P, NC, D])
        yd = at("yd", A0, NC * D, [NB, D])
        hd = at("hd", A0, NC * D + D, [P, KT, NB])

        PS = ctx.enter_context(nc.psum_tensor("PS", [P, 8, 512], fp32))

        def bank(i, n=512, rows=P):
            return PS[0:rows, i, 0:n]

        def bank4(i):
            return PS[:, i, :].rearrange("p (h n) -> p h n", h=H)

        def pj(slot):
            return PS[:, 2 * slot:2 * slot + 2, 0:HC]

        ident = cf[:, C_ID:C_ID + P]
        ones = cf[:, C_ONE:C_ONE + P]
        m_le = cf[:, C_LE:C_LE + P]
        m_gt = cf[:, C_GT:C_GT + P]

        ba8 = ss[0:2 * H]
        vblk = sqb[0:NB].rearrange("p u a n -> p (u a n)")[:, 0:NB * P].rearrange("p (b e) -> p b e", b=NB)
        krow = upd[0:NB].rearrange("p a n -> p (a n)")[:, 0:2 * P].rearrange("p (a e) -> p a e", a=2)

        def states_of(w):
            if w < H:
                return dstate[:, w % 2]
            return (bv, XT, ktok, PT)[w - H][:, 0:2].rearrange("p c h n -> p (c h) n")

        def o_at(i):
            return 3 + 4 * (i % 2)

        def cols_of(i):
            m, c = divmod(i, NC)
            return slice(None), slice(m * H, (m + 1) * H), c // 2, slice((c % 2) * P, (c % 2 + 1) * P)

        def over_heads(m):
            return m.unsqueeze(1).to_broadcast([P, H, P])

        def over_cols(v, n=P):
            return v.unsqueeze(2).to_broadcast([P, v.shape[1], n])

        names = (
            "const_loaded x_loaded param_loaded wba_loaded hist_loaded rope_loaded slab0_loaded slab1_loaded "
            "dstate0_loaded dstate1_loaded dstate2_loaded dstate3_loaded conv_stored state_stored "
            "dstate0_stored dstate1_stored dstate2_stored dstate3_stored y_stored "
            "slab_done x_T param_T hist_T norm_sum ba_done bad_done tail_T stat_done v_T chunk_mm decay_mm "
            "y_mm x_mm ks_mm qs_mm vn_mm od_mm out_T rtr_mm rod_mm dks_mm dkv_T dout_mm do_mm dsum_mm y_T "
            "tile_free x_moved hist_ready h_ready x_ready sq_free wba_ready gate_pre "
            "badiag_ready conv_done crow_ready decay_in bv_ready chunk_used inv_init "
            "y_ready x_new s_ready r_ready vs_ready o_ready osum_ready on_ready catf_ready "
            "rv_ready rs_ready dv_ready dblk_ready dstate_new do_moved dsq_ready catD_ready dcat_ready "
            "a_ready act_ready hd_ready y_moved g_ready "
            "sq_ready rb_ready xh_ready silu_done gates_done gate_exp sqk_ready stat_exp ktok_ready dk_ready "
            "osq_ready orms_ready cath_ready rk_ready gate_silu ah_ready drms_ready dcath_ready "
            "hi_split slab_split mtk_ready s_decayed ds_decayed cat_ready "
            "pool_passed pe_passed dve_passed "
            "dve_step act_step").split()
        s = {n: sem(n) for n in names}

        def alone(eng):
            eng.sem_inc(s[{nc.gpsimd: "pool_passed", nc.tensor: "pe_passed", nc.vector: "dve_passed"}[eng]], 1)

        class Steps:

            def __init__(self, eng, own):
                self.eng, self.own, self.base, self.n, self.outer = eng, own, 0, 0, []

            def __call__(self, ins):
                self.n += 1
                ins.then_inc(self.own, 1)
                self.eng.wait_ge(self.own, self.base + self.n)

            def enter(self, i, per):
                self.outer.append((self.base, self.n, per))
                self.base, self.n = self.base + self.n + i * per, 0

            def leave(self, count):
                base, n, per = self.outer.pop()
                assert self.n == per, (self.n, per)
                self.base, self.n = base, n + count * per

        def split_of(l, n):
            return l * SLABS + n + 1 + NS

        def done_of(l, n):
            return l * SLABS + n + 1 + NW

        def one(ap):
            r = ap.shape
            return ap.rearrange("p o a -> p (o a)") if len(r) == 3 else ap.rearrange("p o a b -> p (o a) b")

        def tile_of(t, k):
            return t[:, bass.ds(k, 1)].rearrange("p o a n -> p (o a) n")

        def halves(ap):
            return ap.rearrange("p (a n) -> p a n", a=2)

        block = ctx.enter_context(nc.Block())

        @block.sync
        def _(sp):
            sp.sem_inc(s["state_stored"], 1)
            sp.dma_start(cf[:], c_f32).then_inc(s["const_loaded"], 16)
            sp.dma_start(mask[:], c_mask).then_inc(s["const_loaded"], 16)
            sp.dma_start(xt[:], x_prompt[0].rearrange("(c p) d -> p c d", p=P)).then_inc(s["x_loaded"], 16)
            sp.dma_start(xd[:], x_sample.rearrange("b o d -> (b o) d")).then_inc(s["x_loaded"], 16)
            with sp.Fori(0, DEPTH) as l:
                def slab(n, slot, cols, rows=(0, KT), w=w_in):
                    sp.wait_ge(s["slab_split"], split_of(l, n) - NS)
                    k0, k1 = rows
                    src = w[bass.ds(l, 1), k0 * P:k1 * P, cols].rearrange("o (k p) n -> p (o k) n", p=P)
                    sp.dma_start(stage[:, slot, 0:k1 - k0, :], src).then_inc(s[f"slab{slot}_loaded"], 16)

                sp.wait_ge(s["param_T"], l + 1)
                for w, r in ((norm_mix_pre, R_MPRE), (norm_mix_post, R_MPOST), (norm_ffn_pre, R_FPRE), (norm_ffn_post, R_FPOST)):
                    sp.dma_start(prows[r:r + KT, :], w[bass.ds(l, 1), :].rearrange("o (k n) -> (o k) n", n=P)).then_inc(s["param_loaded"], 16)
                sp.dma_start(prows[R_CONV:R_GN, :], conv_w[bass.ds(l, 1), :, :].rearrange("o w (t n) -> (o w t) n", n=P)).then_inc(s["param_loaded"], 16)
                sp.dma_start(prows[R_GN:R_GN + 1, :], gdn_norm_w[bass.ds(l, 1), :]).then_inc(s["param_loaded"], 16)
                sp.dma_start(prows[R_RN:R_RN + 1, :], ret_norm_w[bass.ds(l, 1), :]).then_inc(s["param_loaded"], 16)
                sp.wait_ge(s["slab_done"], done_of(l, -1))
                for i, w in enumerate((dt_bias, a_log)):
                    sp.dma_start(adt[:, i, :], w[bass.ds(l, 1), :].to_broadcast([P, H])).then_inc(s["param_loaded"], 16)
                sp.dma_start(wba[:], w_in[bass.ds(l, 1), :, 4 * H * P:4 * H * P + 2 * H].rearrange("o (k p) n -> p (o k) n", p=P)).then_inc(s["wba_loaded"], 16)
                sp.dma_start(hist[:], state_conv[bass.ds(l, 1)].rearrange("o b i n -> (o b i) n")).then_inc(s["hist_loaded"], 16)
                sp.dma_start(rope[:], c_rope).then_inc(s["rope_loaded"], 16)
                sp.dma_start(conv_sample[bass.ds(l, 1), :, 0:CW - 2, :].rearrange("o b i n -> (o b) i n"), state_conv[bass.ds(l, 1), :, 1:CW - 1, :].rearrange("o b i n -> (o b) i n")).then_inc(s["conv_stored"], 16)
                with sp.Fori(0, 4 * H // NS) as i:
                    for u in range(NS):
                        slab(i * NS + u, u, bass.ds((i * NS + u) * P, P))
                with sp.Fori(0, 4 * H // NS) as i:
                    for u in range(NS):
                        slab(i * NS + (u + 4 * H), u, bass.ds((i * NS + u) * P + (4 * H * P + 2 * H), P))
                sp.wait_ge(s["crow_ready"], l + 1)
                sp.dma_start(conv_prompt[bass.ds(l, 1), 0, :, :].rearrange("o i n -> (o i) n"), crow[0:CW - 1, :]).then_inc(s["conv_stored"], 16)
                sp.dma_start(conv_sample[bass.ds(l, 1), :, CW - 2, :].rearrange("o b n -> (o b) n"), crow[CW - 1:CW - 1 + NB, :]).then_inc(s["conv_stored"], 16)
                for u in range(NS):
                    slab(u + S_OUT, u, slice(u * P, (u + 1) * P), w=w_out)

                def load_states(w):
                    st = state_gdn if w < H else state_ret
                    sp.dma_start(states_of(w), st[bass.ds(l, 1), :, w % H, :, :].rearrange("o b d e -> d (o b) e")).then_inc(s[f"dstate{w % 4}_loaded"], 16)

                sp.wait_ge(s["slab_done"], done_of(l, IN_T - 1))
                for w in range(2):
                    load_states(w)
                for w in range(2 * H):
                    st = gdn_sample if w < H else ret_sample
                    sp.wait_ge(s["dstate_new"], l * 2 * H + (w + 1))
                    sp.dma_start(st[bass.ds(l, 1), :, w % H, :, :].rearrange("o b d e -> d (o b) e"), states_of(w)).then_inc(s[f"dstate{w % 4}_stored"], 16)
                    if w + 2 < H:
                        sp.wait_ge(s[f"dstate{w % 4}_stored"], (l * 2 + 1) * 16)
                        sp.wait_ge(s["do_mm"], l * 2 * H + (w + 1))
                        load_states(w + 2)
                    if w == 2:
                        sp.wait_ge(s["o_ready"], l * 2 * NC + 2)
                        for v in range(H, 2 * H - 1):
                            load_states(v)
                    if w == 3:
                        load_states(2 * H - 1)
                with sp.Fori(1, OUT_T // NS) as i:
                    for u in range(NS):
                        slab(i * NS + (u + S_OUT), u, bass.ds((i * NS + u) * P, P), w=w_out)
                sp.wait_ge(s["s_ready"], (l + 1) * (NC + 1))
                sp.dma_start(gdn_prompt[bass.ds(l, 1), 0].rearrange("o h d e -> d (o h) e"), S[:]).then_inc(s["state_stored"], 16)
                sp.wait_ge(s["rs_ready"], (l + 1) * (NC + 1))
                sp.dma_start(ret_prompt[bass.ds(l, 1), 0].rearrange("o h d e -> d (o h) e"), Sr[:]).then_inc(s["state_stored"], 16)
                with sp.Fori(0, FT) as i:
                    for u in range(2):
                        slab(i * 2 + (u + S_GU), u, bass.ds(i * P + u * FT * P, P), w=w_gate_up)
                with sp.Fori(0, KT) as i:
                    k = 0
                    for u, n in enumerate(PIECES):
                        slab(i * len(PIECES) + (u + S_DN), u % NS, bass.ds(i * P, P), rows=(k, k + n), w=w_down)
                        k += n
            for c in range(NC):
                sp.wait_ge(s["y_moved"], c + 1)
                sp.dma_start(y_prompt[0, c * P:(c + 1) * P, :], ytok[:, c, :]).then_inc(s["y_stored"], 16)
            sp.wait_ge(s["y_moved"], NC + 1)
            sp.dma_start(y_sample.rearrange("b o d -> (b o) d"), yd[:]).then_inc(s["y_stored"], 16)
            sp.wait_ge(s["conv_stored"], DEPTH * 48)
            sp.wait_ge(s["state_stored"], DEPTH * 32 + 1)
            for w in range(4):
                sp.wait_ge(s[f"dstate{w}_stored"], DEPTH * 2 * H // 4 * 16)
            sp.wait_ge(s["y_stored"], 16 * (NC + 1))

        @block.gpsimd
        def _(pool):
            pool.sem_inc(s["slab_split"], NS)
            with pool.Fori(0, DEPTH) as l:
                def split(r, slot, k=KT):
                    n = r * NS + slot
                    pool.wait_ge(s[f"slab{slot}_loaded"], (l * (SLABS // NS) + r + 1) * 16)
                    pool.wait_ge(s["slab_done"], done_of(l, n) - NW)
                    alone(pool)
                    nc.gpsimd.tensor_scalar(Wh[:, slot, 0:k, :], stage[:, slot, 0:k, :], 1.0, 1.0, ALU.mult, ALU.mult).then_inc(s["hi_split"], 1)
                    pool.wait_ge(s["hi_split"], l * SLABS + n + 1)
                    nc.gpsimd.tensor_tensor(Wl[:, slot, 0:k, :], stage[:, slot, 0:k, :], Wh[:, slot, 0:k, :].bitcast(fp32), ALU.subtract).then_inc(s["slab_split"], 1)
                    pool.wait_ge(s["slab_split"], split_of(l, n))

                alone(pool)
                with pool.Fori(0, IN_T // NS) as i:
                    for u in range(NS):
                        split(i, u)
                pool.wait_ge(s["conv_done"], (l + 1) * QKV)
                pool.wait_ge(s["slab_done"], done_of(l, IN_T - 1))
                alone(pool)
                for x in (XT, Xinv):
                    nc.gpsimd.tensor_copy(x[:].rearrange("p c h n -> p (c h) n"), ident.unsqueeze(1).to_broadcast([P, NC * H, P])).then_inc(s["inv_init"], 1)
                pool.wait_ge(s["chunk_used"], (l + 1) * NC)
                alone(pool)
                with pool.Fori(0, LEVELS) as k:
                    for c in range(NC):
                        n = l * (LEVELS * NC) + k * NC + c
                        pool.wait_ge(s["y_mm"], n + 1)
                        alone(pool)
                        mk = mask[:, bass.ds(k, 1), :].to_broadcast([P, H, P])
                        nc.gpsimd.tensor_tensor(T[:, c % 2], MT[:, c], mk, ALU.mult).then_inc(s["mtk_ready"], 1)
                        pool.wait_ge(s["mtk_ready"], n + 1)

                def rest_cat(i):
                    n = l * 2 * NC + i
                    pool.wait_ge(s["cath_ready"], n + 1)
                    if i == NC:
                        for w in range(4):
                            pool.wait_ge(s[f"dstate{w}_stored"], (l * 2 + 1) * 16)
                    nc.gpsimd.tensor_tensor(Xl[cols_of(i)], T[:, 6], Xh[cols_of(i)].bitcast(fp32), ALU.subtract).then_inc(s["cat_ready"], 1)
                    pool.wait_ge(s["cat_ready"], n + 1)

                for i in range(2 * NC):
                    if i < NC:
                        pool.wait_ge(s["qs_mm"], l * NC + i + 1)
                        nc.gpsimd.tensor_tensor(S[:], S[:], over_cols(egc[:, 1, i, :]), ALU.mult).then_inc(s["s_decayed"], 1)
                        pool.wait_ge(s["dks_mm"], l * H + i + 1)
                        nc.gpsimd.tensor_tensor(states_of(i), states_of(i), over_cols(adec[:, :, i]), ALU.mult).then_inc(s["ds_decayed"], 1)
                    if i:
                        rest_cat(i - 1)
                rest_cat(2 * NC - 1)
                alone(pool)
                with pool.Fori(0, (OUT_T + GU_T) // NS) as i:
                    for u in range(NS):
                        split(i + S_OUT // NS, u)
                alone(pool)
                with pool.Fori(0, KT) as i:
                    for u, n in enumerate(PIECES):
                        split(i * (len(PIECES) // NS) + (u + S_DN) // NS, u % NS, n)

        @block.tensor
        def _(pe):
            mm, tr = nc.tensor.matmul, nc.tensor.transpose
            pe.sem_inc(s["slab_done"], NW)
            pe.sem_inc(s["y_mm"], 2)
            pe.sem_inc(s["param_T"], 1)
            pe.sem_inc(s["norm_sum"], 1)
            pe.wait_ge(s["const_loaded"], 32)
            pe.wait_ge(s["x_loaded"], 32)
            for k in range(KT):
                if k >= 4:
                    pe.wait_ge(s["x_moved"], k - 3)
                for c in range(NC):
                    last = tr(PS[:, k % 4, c * P:(c + 1) * P], xt[:, c, k * P:(k + 1) * P], ident)
                last.then_inc(s["x_T"], 1)
            for k in range(KT):
                last = tr(PS[:, 4, k * NB:(k + 1) * NB], xd[:, k * P:(k + 1) * P], cf[0:NB, C_ID:C_ID + NB])
            last.then_inc(s["x_T"], 1)
            pe.wait_ge(s["x_moved"], KT + 2)

            with pe.Fori(0, DEPTH) as l:
                def project(n, t, slot, x, k0=0, k=KT, first=True, end=True, wslot=None):
                    wslot = slot if wslot is None else wslot
                    pe.wait_ge(s["slab_split"], split_of(l, n))
                    if first:
                        pe.wait_ge(s["tile_free"], l * TILES + t + 1)
                    xh, xl = x
                    for j in range(k):
                        for w, xx in ((Wh, xh), (Wh, xl), (Wl, xh)):
                            for half in range(2):
                                go = first and j == 0 and w is Wh and xx is xh
                                stop = end and j == k - 1 and w is Wl
                                last = mm(PS[:, 2 * slot + half, 0:HC], w[:, wslot, j, :], xx[:, k0 + j, half, :], start=go, stop=stop)
                    last.then_inc(s["slab_done"], 1)

                def norm_sum(n):
                    pe.wait_ge(s["sq_free"], (l * 4 + n + 1) * KT + 2)
                    for half in range(2):
                        last = mm(PS[:, 4 + half, 0:HC], ones, ss[:, half, :], start=True, stop=True)
                    last.then_inc(s["norm_sum"], 1)

                def project_first(n, s0, t0):
                    def add_sums(k):
                        pe.wait_ge(s["sq_ready"], (l * 4 + n) * KT + (k + 1))
                        for half in range(2):
                            last = mm(PS[:, 4 + half, 0:HC], ones, sqb[:, k % 2, half, :], start=k == 0, stop=k == KT - 1)
                        last.then_inc(s["sq_free"], 1)

                    if n == 0:
                        for k in range(KT):
                            add_sums(k)
                    for u in range(2):
                        pe.wait_ge(s["slab_split"], split_of(l, s0 + u))
                        pe.wait_ge(s["tile_free"], l * TILES + (t0 + u + 1))
                    for k in range(KT):
                        pe.wait_ge(s["x_ready"], l * 2 * KT + (k + 1 + (KT if n else 0)))
                        for u in range(2):
                            for w, xx in ((Wh, Xh), (Wh, Xl), (Wl, Xh)):
                                for half in range(2):
                                    last = mm(PS[:, 2 * u + half, 0:HC], w[:, u, k, :], xx[:, k, half, :], start=k == 0 and w is Wh and xx is Xh, stop=k == KT - 1 and w is Wl)
                            if k == KT - 1:
                                last.then_inc(s["slab_done"], 1)
                        if n:
                            add_sums(k)

                pe.wait_ge(s["param_loaded"], (l + 1) * 9 * 16)
                tr(PS[:, 6, 0:NR], prows[:], cf[0:NR, C_ID:C_ID + NR]).then_inc(s["param_T"], 1)
                pe.wait_ge(s["hist_loaded"], (l + 1) * 16)
                alone(pe)
                nh = NB * (CW - 1)
                for t in range(QKV):
                    last = tr(PS[:, 7, t * nh:(t + 1) * nh], hist[:, t * P:(t + 1) * P], cf[0:nh, C_ID:C_ID + nh])
                last.then_inc(s["hist_T"], 1)

                X = (Xh, Xl)
                project_first(0, 0, 0)
                pe.wait_ge(s["wba_ready"], l + 1)
                pe.wait_ge(s["hist_ready"], l + 1)
                for half in range(2):
                    for j in range(KT):
                        last = mm(PS[0:2 * H, 6 + half, 0:HC], wba[:, j, :], hT[:, j, half, :], start=j == 0, stop=j == KT - 1)
                last.then_inc(s["ba_done"], 1)
                def project_tiles(t0, t1):
                    alone(pe)
                    with pe.Fori(0, (t1 - t0) // 2) as i:
                        for u in range(2):
                            n = i * 2 + (u + t0)
                            project(n, n, u, X)

                project_tiles(2, 4 * H)
                pe.wait_ge(s["badiag_ready"], l + 1)
                alone(pe)
                for c in range(NC):
                    tr(PS[:, 7, c * 2 * H:(c + 1) * 2 * H], ba8[:, c // 2, (c % 2) * P:(c % 2 + 1) * P], cf[0:2 * H, C_ID:C_ID + 2 * H])
                mm(PS[:, 6, 64:64 + NB * 2 * H], cf[0:2 * H, C_ONE:C_ONE + P], bad[:].rearrange("a b n -> a (b n)"), start=True, stop=True).then_inc(s["bad_done"], 1)
                pe.wait_ge(s["sqk_ready"], (l + 1) * 2 * H)
                for c in range(NC):
                    for t in range(2 * H):
                        mm(PS[:, 5, c * 2 * H + t:c * 2 * H + t + 1], sqk[:, t, c * P:(c + 1) * P], ones[:, 0:1], start=True, stop=True)
                mm(PS[:, 5, 128:128 + 2 * H * NB], ones, sqd[:].rearrange("p a b -> p (a b)"), start=True, stop=True)
                project_tiles(4 * H, 7 * H)
                pe.wait_ge(s["g_ready"], l + 1)
                gp_ = g[:, 0:NC, :].rearrange("p c h -> p (c h)")
                mm(PS[:, 5, 64:64 + NC * H], m_le, gp_, start=True, stop=True)
                mm(PS[:, 5, 80:80 + NC * H], ones, gp_, start=True, stop=True).then_inc(s["stat_done"], 1)
                project_tiles(7 * H, IN_T)

                pe.wait_ge(s["stat_exp"], l + 1)
                pe.wait_ge(s["conv_done"], (l + 1) * QKV)
                nt = CW - 1 + NB
                for t in range(QKV):
                    last = tr(PS[0:nt, 4 + t // 4, (t % 4) * P:(t % 4 + 1) * P], tailT[:, t, :], ident)
                last.then_inc(s["tail_T"], 1)

                pe.wait_ge(s["tile_free"], l * TILES + IN_T + 2)
                for c in range(NC):
                    for h in range(H):
                        last = tr(PS[:, c, h * P:(h + 1) * P], qkvT[:, 2 * H + h, c * P:(c + 1) * P], ident)
                last.then_inc(s["v_T"], 1)
                for c in range(NC):
                    b0 = 4 * (1 - c % 2)
                    if c == 0:
                        pe.wait_ge(s["crow_ready"], l + 1)
                    if c == 1:
                        pe.wait_ge(s["bv_ready"], l + 1)
                    if c >= 2:
                        pe.wait_ge(s["chunk_used"], l * NC + c - 1)
                        pe.wait_ge(s["ktok_ready"], l * NC + c - 1)
                    cs = slice(c * P, (c + 1) * P)
                    for h in range(H):
                        tr(PS[:, b0, h * P:(h + 1) * P], qkvT[:, H + h, cs], ident)
                    for h in range(H):
                        mm(PS[:, b0 + 1, h * P:(h + 1) * P], qkvT[:, H + h, cs], qkvT[:, H + h, cs], start=True, stop=True)
                    for h in range(H):
                        last = mm(PS[:, b0 + 2, h * P:(h + 1) * P], qkvT[:, H + h, cs], qkvT[:, h, cs], start=True, stop=True)
                    last.then_inc(s["chunk_mm"], 1)
                    pe.wait_ge(s["decay_in"], l * NC + c + 1)
                    for h in range(H):
                        last = mm(PS[:, b0 + 3, h * P:(h + 1) * P], T[:, c % 2, h, :], m_le, start=True, stop=True)
                    last.then_inc(s["decay_mm"], 1)

                pe.wait_ge(s["inv_init"], (l + 1) * 2)
                pe.wait_ge(s["ktok_ready"], (l + 1) * NC)
                def level(m, first=False, last_level=False):
                    def left(c):
                        pe.wait_ge(s["x_new"], m + (c + 1))
                        pe.wait_ge(s["mtk_ready"], m + (c + 1))
                        for h in range(H):
                            to = PS[:, c, h * P:(h + 1) * P]
                            last = tr(to, T[:, c % 2, h, :], ident) if first else mm(to, T[:, c % 2, h, :], Xinv[:, c, h, :], start=True, stop=True)
                        last.then_inc(s["y_mm"], 1)

                    def right(c):
                        pe.wait_ge(s["y_ready"], m + (c + 1))
                        pe.wait_ge(s["x_new"], m + (c + 3))
                        if not (first or last_level):
                            for h in range(H):
                                mm(PS[:, 4 + c % 2, h * P:(h + 1) * P], XT[:, c, h, :], T[:, 2 + c % 2, h, :], start=True, stop=True)
                        for h in range(H):
                            to = PS[:, 6 + c % 2, h * P:(h + 1) * P]
                            last = tr(to, T[:, 2 + c % 2, h, :], ident) if first else mm(to, T[:, 2 + c % 2, h, :], XT[:, c, h, :], start=True, stop=True)
                        last.then_inc(s["x_mm"], 1)

                    left(0)
                    for c in range(1, NC):
                        left(c)
                        right(c - 1)
                    right(NC - 1)

                level(l * (LEVELS * NC), first=True)
                alone(pe)
                with pe.Fori(0, LEVELS - 2) as k:
                    level(l * (LEVELS * NC) + k * NC + NC)
                level(l * (LEVELS * NC) + (LEVELS - 1) * NC, last_level=True)

                def out_rows(n):
                    pe.wait_ge(s["on_ready"], n + 1)
                    for h in range(H):
                        last = tr(PS[:, 5, h * P:(h + 1) * P], T[:, 4, h, :], ident)
                    last.then_inc(s["out_T"], 1)

                def sample_keys(w):
                    if w:
                        pe.wait_ge(s["do_moved"], l * 2 * H + w)
                    pe.wait_ge(s[f"dstate{w % 4}_loaded"], (l * 2 + (w // 4 + 1)) * 16)
                    if w < H:
                        for b in range(NB):
                            last = mm(PS[:, 2, b:b + 1], states_of(w)[:, b, :], qkvD[:, H + w, b:b + 1], start=True, stop=True)
                        last.then_inc(s["dks_mm"], 1)

                def sample_rows(w):
                    pe.wait_ge(s["dv_ready"], l * 2 * H + (w + 1))
                    tr(PS[0:NB, 2, P:2 * P], qkvD[:, H + w, :] if w < H else rD[:, w, :], ident)
                    tr(PS[0:NB, 2, 2 * P:3 * P], du[:], ident).then_inc(s["dkv_T"], 1)

                def sample_outer(w):
                    pe.wait_ge(s["dblk_ready"], l * 2 * H + (w + 1))
                    for half in range(2):
                        last = mm(bank(6 + half), krow[:, 0, :], vblk[:, half * NB // 2:(half + 1) * NB // 2, :].rearrange("a b e -> a (b e)"), start=True, stop=True)
                    last.then_inc(s["dout_mm"], 1)

                def sample_read(w):
                    pe.wait_ge(s["dstate_new"], l * 2 * H + (w + 1))
                    for b in range(NB):
                        last = mm(PS[:, 2, 3 * P + b:3 * P + b + 1], states_of(w)[:, b, :], (qkvD[:, w, :] if w < H else rD[:, w - H, :])[:, b:b + 1], start=True, stop=True)
                    last.then_inc(s["do_mm"], 1)

                pe.wait_ge(s["x_new"], (l + 1) * (LEVELS * NC) + 4)
                for c in range(NC):
                    cs = slice(c * P, (c + 1) * P)
                    pe.wait_ge(s["s_ready"], l * (NC + 1) + c + 1)
                    for h in range(H):
                        last = mm(PS[:, 0, h * P:(h + 1) * P], qkvT[:, H + h, cs], S[:, h, :], start=True, stop=True)
                    last.then_inc(s["ks_mm"], 1)
                    for h in range(H):
                        last = mm(PS[:, 1, h * P:(h + 1) * P], qkvT[:, h, cs], S[:, h, :], start=True, stop=True)
                    last.then_inc(s["qs_mm"], 1)
                    if c:
                        sample_read(c - 1)
                    pe.wait_ge(s["r_ready"], l * NC + c + 1)
                    for h in range(H):
                        last = mm(PS[:, 0, h * P:(h + 1) * P], XT[:, c, h, :], T[:, 0, h, :], start=True, stop=True)
                    last.then_inc(s["vn_mm"], 1)
                    sample_keys(c)
                    if c:
                        out_rows(l * 2 * NC + c - 1)
                    sample_rows(c)
                    pe.wait_ge(s["vs_ready"], l * NC + c + 1)
                    for h in range(H):
                        mm(PS[:, 3, h * P:(h + 1) * P], PT[:, c, h, :], T[:, 1, h, :], start=True, stop=True)
                    for h in range(H):
                        last = mm(PS[:, 4, h * P:(h + 1) * P], ktok[:, c, h, :], T[:, 2, h, :], start=True, stop=True)
                    last.then_inc(s["od_mm"], 1)
                    sample_outer(c)

                for c in range(NC):
                    cs = slice(c * P, (c + 1) * P)
                    if c == 0:
                        pe.wait_ge(s["s_ready"], (l + 1) * (NC + 1))
                        pe.wait_ge(s["o_ready"], l * 2 * NC + NC)
                    pe.wait_ge(s["rs_ready"], l * (NC + 1) + c + 1)
                    for h in range(H):
                        tr(PS[:, 0, h * P:(h + 1) * P], rT[:, H + h, cs], ident)
                    for h in range(H):
                        tr(PS[:, 1, h * P:(h + 1) * P], rT[:, 2 * H + h, cs], ident)
                    for h in range(H):
                        last = mm(PS[:, 3, h * P:(h + 1) * P], rT[:, H + h, cs], rT[:, h, cs], start=True, stop=True)
                    last.then_inc(s["rtr_mm"], 1)
                    sample_read(H + c - 1)
                    sample_keys(H + c)
                    sample_rows(H + c)
                    pe.wait_ge(s["rk_ready"], l * NC + c + 1)
                    pe.wait_ge(s["rv_ready"], l * NC + c + 1)
                    for h in range(H):
                        mm(PS[:, 4, h * P:(h + 1) * P], rT[:, h, cs], Sr[:, h, :], start=True, stop=False)
                        mm(PS[:, 4, h * P:(h + 1) * P], T[:, 2, h, :], T[:, 1, h, :], start=False, stop=True)
                    for h in range(H):
                        last = mm(PS[:, 0, h * P:(h + 1) * P], T[:, 0, h, :], T[:, 1, h, :], start=True, stop=True)
                    last.then_inc(s["rod_mm"], 1)
                    out_rows(l * 2 * NC + NC + c - 1)
                    sample_outer(H + c)
                sample_read(2 * H - 1)
                pe.wait_ge(s["dsq_ready"], l + 1)
                mm(PS[:, 2, 0:2 * H * NB], ones, dn[:].rearrange("p a b -> p (a b)"), start=True, stop=True).then_inc(s["dsum_mm"], 1)
                out_rows(l * 2 * NC + 2 * NC - 1)

                pe.wait_ge(s["cat_ready"], (l + 1) * 2 * NC)
                pe.wait_ge(s["dcat_ready"], l + 1)
                alone(pe)
                with pe.Fori(0, OUT_T // 2) as i:
                    for u in range(2):
                        n = i * 2 + u
                        project(n + S_OUT, n + T_OUT, u, X)
                norm_sum(1)

                project_first(2, S_GU, T_GU)
                alone(pe)
                with pe.Fori(0, FT - 1) as i:
                    for u in range(2):
                        n = i * 2 + (u + 2)
                        project(n + S_GU, n + T_GU, u, X)
                alone(pe)
                with pe.Fori(0, KT // 2) as i:
                    for u in range(2):
                        k0 = 0
                        for q, k in enumerate(PIECES):
                            n = i * 2 * len(PIECES) + (u * len(PIECES) + q)
                            last_piece = q == len(PIECES) - 1
                            if u == 0:
                                pe.wait_ge(s["act_ready"], l * FT + (k0 + k))
                            project(n + S_DN, i * 2 + (u + T_DN), u, (actH, actL), k0=k0, k=k, first=q == 0, end=last_piece, wslot=q % NW)
                            k0 += k
                norm_sum(3)

            pe.wait_ge(s["h_ready"], KT + DEPTH * 2 * KT)
            pe.wait_ge(s["hd_ready"], 1)
            for c in range(NC):
                if c >= 2:
                    pe.wait_ge(s["y_moved"], c - 1)
                for k in range(KT):
                    last = tr(PS[:, 2 * (c % 2) + k // 4, (k % 4) * P:(k % 4 + 1) * P], hT[:, k, c // 2, (c % 2) * P:(c % 2 + 1) * P], ident)
                last.then_inc(s["y_T"], 1)
            for k in range(KT):
                last = tr(PS[0:NB, 4 + k // 4, (k % 4) * P:(k % 4 + 1) * P], hd[:, k, :], ident)
            last.then_inc(s["y_T"], 1)

        SC = float(P) ** -0.5
        WIN = CW - 1 + SEQ

        @block.scalar
        def _(act):
            A = nc.scalar.activation
            step = Steps(act, s["act_step"])

            def sig(ins, name, count):
                ins.then_inc(s[name], 1)
                act.wait_ge(s[name], count)

            act.sem_inc(s["silu_done"], 2)
            act.sem_inc(s["rb_ready"], 1)
            act.wait_ge(s["const_loaded"], 32)
            with act.Fori(0, DEPTH) as l:
                step.enter(l, ACT_STEPS)

                def square(n, k, src, slot):
                    act.wait_ge(s["sq_free"], (l * 4 + n) * KT + k + 1)
                    sig(A(sqb[:, slot], src, ACT.Square), "sq_ready", (l * 4 + n) * KT + k + 1)

                def rsqrt_mean(n):
                    if n % 2:
                        act.wait_ge(s["norm_sum"], l * 2 + (n // 2 + 2))
                    else:
                        act.wait_ge(s["sq_free"], (l * 4 + n + 1) * KT + 2)
                    step(A(rb[:], PS[:, 4:6, 0:HC], ACT.Ln, scale=1.0 / D, bias=EPS))
                    sig(A(rb[:], rb[:], ACT.Exp, scale=-0.5), "rb_ready", l * 4 + n + 2)

                def prepare(n, row):
                    first = l * 2 * KT + (KT if n else 0)
                    if n == 0:
                        for k in range(KT):
                            act.wait_ge(s["h_ready"], first + k + 1)
                            square(n, k, hT[:, k], k % 2)
                        act.wait_ge(s["hist_ready"], l + 1)
                    for k in range(KT):
                        if n:
                            act.wait_ge(s["h_ready"], first + k + 1)
                        sig(A(Xh[:, k], hT[:, k], ACT.Copy, scale=prm[:, row + k:row + k + 1]), "xh_ready", first + k + 1)
                        if n:
                            square(n, k, hT[:, k], k % 2)
                        elif k == KT // 2 - 1:
                            rsqrt_mean(0)
                    if n:
                        rsqrt_mean(n)

                prepare(0, R_MPRE)
                def silu_tiles(t0, t1, squares):
                    with act.Fori(0, (t1 - t0) // 2) as i:
                        step.enter(i, 4 if squares else 2)
                        for u in range(2):
                            n = i * 2 + (u + t0)
                            act.wait_ge(s["conv_done"], l * QKV + n + 1)
                            vT, vD = one(qkvT[:, bass.ds(n, 1), :]), one(qkvD[:, bass.ds(n, 1), :])
                            step(A(vT, conv[:, u, 0:SEQ], ACT.Silu))
                            sig(A(vD, conv[:, u, WIN:CONV_N:CW], ACT.Silu), "silu_done", l * QKV + n + 3)
                            if squares:
                                step(A(one(sqk[:, bass.ds(n, 1), :]), vT, ACT.Square))
                                sig(A(one(sqd[:, bass.ds(n, 1), :]), vD, ACT.Square), "sqk_ready", l * 2 * H + n + 1)
                        step.leave((t1 - t0) // 2)

                act.wait_ge(s["hist_T"], l + 1)
                silu_tiles(0, 2 * H, True)
                silu_tiles(2 * H, QKV, False)
                act.wait_ge(s["gate_pre"], l + 1)
                step(A(gb[:], ga[:, :, 0:H], ACT.Exp, scale=-1.0))
                step(A(adt[:, 1, :], adt[:, 1, :], ACT.Exp))
                step(A(gs[:], gs[:], ACT.Exp, scale=-1.0))
                sig(A(gs[:], gs[:], ACT.Ln, bias=1.0), "gate_exp", l + 1)
                act.wait_ge(s["stat_done"], l + 1)
                step(A(lrq[:].rearrange("p c h -> p (c h)"), PS[:, 5, 0:NC * 2 * H], ACT.Ln, bias=L2_EPS))
                step(A(rqd[:].rearrange("p h b -> p (h b)"), PS[:, 5, 128:128 + 2 * H * NB], ACT.Ln, bias=L2_EPS))
                step(A(rqd[:], rqd[:], ACT.Exp, scale=-0.5))
                step(A(rq[:], lrq[:], ACT.Exp, scale=-0.5))
                step(A(lrq[:], lrq[:], ACT.Copy, scale=-0.5))
                step(A(adec[:], g[:, NC:NG, :], ACT.Exp))
                sig(A(egc[:].rearrange("p a c h -> p (a c h)"), PS[:, 5, 64:64 + 2 * NC * H], ACT.Exp), "stat_exp", l + 1)
                for c in range(NC):
                    n = l * NC + c
                    act.wait_ge(s["chunk_mm"], n + 1)
                    sig(A(ktok[:, c], bank4(4 * (1 - c % 2)), ACT.Copy), "ktok_ready", n + 1)
                    act.wait_ge(s["decay_mm"], n + 1)
                    if c >= 2:
                        act.wait_ge(s["chunk_used"], n - 1)
                    for h in range(H):
                        ins = A(T[:, 2 + c % 2, h, :], PS[:, 4 * (1 - c % 2) + 3, h * P:(h + 1) * P], ACT.Exp, bias=lrq[:, c, H + h:H + h + 1])
                        if h < H - 1:
                            step(ins)
                        else:
                            sig(ins, "dk_ready", n + 1)

                act.wait_ge(s["tile_free"], l * TILES + IN_T + 2)
                sig(A(gates[:], gates[:], ACT.Silu), "gates_done", l + 1)

                def row_norms(i):
                    n = l * 2 * NC + i
                    act.wait_ge(s["o_ready"], n + 1)
                    for h in range(H):
                        ins = A(T[:, 5, h, :], T[:, o_at(i), h, :], ACT.Square, accum_out=nrm[:, 0, h:h + 1])
                        if h < H - 1:
                            step(ins)
                        else:
                            sig(ins, "osq_ready", n + 1)
                    act.wait_ge(s["osum_ready"], n + 1)
                    step(A(nrm[:, 2, :], nrm[:, 1, :], ACT.Ln, scale=1.0 / P, bias=EPS))
                    if i == 2 * NC - 1:
                        act.wait_ge(s["dsum_mm"], l + 1)
                        step(A(drm[:].rearrange("p h b -> p (h b)"), PS[:, 2, 0:2 * H * NB], ACT.Ln, scale=1.0 / P, bias=EPS))
                        sig(A(drm[:], drm[:], ACT.Exp, scale=-0.5), "drms_ready", l + 1)
                    sig(A(nrm[:, 2, :], nrm[:, 2, :], ACT.Exp, scale=-0.5), "orms_ready", n + 1)

                def round_cat(i):
                    n = l * 2 * NC + i
                    m, c = divmod(i, NC)
                    act.wait_ge(s["catf_ready"], n + 1)
                    if i == 0:
                        act.wait_ge(s["conv_stored"], (l + 1) * 48)
                    dst = Xh[:, m * H:(m + 1) * H, c // 2, (c % 2) * P:(c % 2 + 1) * P]
                    sig(A(dst, T[:, 6], ACT.Copy), "cath_ready", n + 1)

                for i in range(2 * NC):
                    if i >= NC:
                        act.wait_ge(s["rtr_mm"], l * NC + (i - NC + 1))
                        sig(A(T[:, 0], bank4(0), ACT.Copy), "rk_ready", l * NC + (i - NC + 1))
                    if i:
                        round_cat(i - 1)
                    row_norms(i)
                act.wait_ge(s["catD_ready"], l + 1)
                dec = Xh[:].rearrange("p k a n -> p (k a) n")[:, :, HALF:HC]
                sig(A(dec, catD[:].rearrange("p h (a b) -> p (h a) b", a=2), ACT.Copy), "dcath_ready", l + 1)
                round_cat(2 * NC - 1)

                def squares_of(n, t0, src):
                    with act.Fori(0, KT // 2) as i:
                        for u in range(2):
                            k = i * 2 + u
                            act.wait_ge(s["tile_free"], l * TILES + k + (t0 + 3))
                            square(n, k, tile_of(src, k), u)
                    rsqrt_mean(n)

                squares_of(1, T_OUT, mT)
                prepare(2, R_FPRE)
                with act.Fori(0, FT // 2) as i:
                    for u in range(2):
                        j = i * 2 + u
                        act.wait_ge(s["tile_free"], l * TILES + j * 2 + (T_GU + 3))
                        sig(A(gp[:, u], gp[:, u], ACT.Silu), "gate_silu", l * FT + j + 1)
                        act.wait_ge(s["a_ready"], l * FT + j + 1)
                        sig(A(tile_of(actH, j), ab[:, u], ACT.Copy), "ah_ready", l * FT + j + 1)
                squares_of(3, T_DN, fT)
                step.leave(DEPTH)

        @block.vector
        def _(dve):
            V = nc.vector
            step = Steps(dve, s["dve_step"])

            def sig(ins, name, count):
                ins.then_inc(s[name], 1)
                dve.wait_ge(s[name], count)

            dve.sem_inc(s["tile_free"], 2)
            dve.sem_inc(s["sq_free"], 2)
            dve.sem_inc(s["x_new"], 4)
            dve.wait_ge(s["const_loaded"], 32)
            for k in range(KT):
                dve.wait_ge(s["x_T"], k + 1)
                sig(V.tensor_copy(hT[:, k, :, 0:HALF], PS[:, k % 4, :].rearrange("p (a n) -> p a n", a=2)), "x_moved", k + 1)
            dve.wait_ge(s["x_T"], KT + 1)
            for a in range(2):
                src = PS[:, 4, 0:KT * NB].rearrange("p (k b) -> p k b", k=KT)[:, :, a * NBH:(a + 1) * NBH]
                sig(V.tensor_copy(hT[:, :, a, HALF:HC], src), "x_moved", KT + 1 + a)
            dve.sem_inc(s["h_ready"], KT)

            with dve.Fori(0, DEPTH) as l:
                step.enter(l, DVE_STEPS)

                def add_squares(n, k, slot):
                    dve.wait_ge(s["sq_ready"], (l * 4 + n) * KT + k + 1)
                    sig(V.tensor_tensor(ss[:], ss[:], sqb[:, slot], ALU.add), "sq_free", (l * 4 + n) * KT + k + 3)

                def rest_x(n, k, row):
                    count = l * 2 * KT + ((KT if n else 0) + k + 1)
                    dve.wait_ge(s["xh_ready"], count)
                    sig(V.scalar_tensor_tensor(Xl[:, k], hT[:, k], prm[:, row + k:row + k + 1], Xh[:, k].bitcast(fp32), ALU.mult, ALU.subtract), "x_ready", count)

                def tile_done(t):
                    dve.wait_ge(s["slab_done"], l * SLABS + t + (1 + NW))

                def moved(ins, t):
                    sig(ins, "tile_free", l * TILES + t + 3)

                dve.wait_ge(s["param_T"], l + 2)
                step(V.tensor_copy(prm[:], PS[:, 6, 0:NR]))
                dve.wait_ge(s["hist_T"], l + 1)
                sig(V.tensor_copy(histT[:].rearrange("p t b i -> p (t b i)"), PS[:, 7, 0:QKV * NB * (CW - 1)]), "hist_ready", l + 1)
                wpre = prm[:, R_MPRE:R_MPRE + KT].unsqueeze(2).to_broadcast([P, KT, 2 * H])
                for k in range(KT):
                    rest_x(0, k, R_MPRE)
                dve.wait_ge(s["wba_loaded"], (l + 1) * 16)
                sig(V.tensor_tensor(wba[:], wba[:], wpre, ALU.mult), "wba_ready", l + 1)
                step(V.memset(raw[:, :, 0:CW - 1], 0.0))
                dve.wait_ge(s["state_stored"], l * 32 + 1)
                sig(V.memset(S[:], 0.0), "s_ready", l * (NC + 1) + 1)
                sig(V.memset(Sr[:], 0.0), "rs_ready", l * (NC + 1) + 1)
                dve.wait_ge(s["ba_done"], l + 1)
                dve.wait_ge(s["rb_ready"], l * 4 + 2)
                eye_rows = cf[0:NB, C_ID:C_ID + NB]
                step(V.tensor_tensor(ba8[:], PS[0:2 * H, 6:8, 0:HC], rb[0:2 * H], ALU.mult))
                for a in range(2):
                    ins = V.tensor_tensor(bad[:, a * NBH:(a + 1) * NBH], ba8[:, a, HALF:HC].unsqueeze(2).to_broadcast([2 * H, NBH, 2 * H]), cf[0:2 * H, C_ID:C_ID + 2 * H].unsqueeze(1).to_broadcast([2 * H, NBH, 2 * H]), ALU.mult)
                    if a == 0:
                        step(ins)
                    else:
                        sig(ins, "badiag_ready", l + 1)

                alone(dve)
                with dve.Fori(0, QKV // 2) as i:
                    step.enter(i, 2 * (4 + CW - 1))
                    for u in range(2):
                        t = i * 2 + u
                        tile_done(t)
                        win = raw[:, u, WIN:RAW].rearrange("p (b w) -> p b w", w=CW)
                        step(V.tensor_tensor(raw[:, u, CW - 1:WIN].rearrange("p (a n) -> p a n", a=2), pj(u)[:, :, 0:HALF], rb[:, :, 0:HALF], ALU.mult))
                        moved(V.tensor_tensor(win[:, :, CW - 1].rearrange("p (a b) -> p a b", a=2), pj(u)[:, :, HALF:HC], rb[:, :, HALF:HC], ALU.mult), t)
                        step(V.tensor_copy(win[:, :, 0:CW - 1], one(histT[:, bass.ds(t, 1)])))
                        step(V.tensor_copy(one(tailT[:, bass.ds(t, 1), 0:CW - 1]), raw[:, u, SEQ:WIN]))
                        step(V.tensor_copy(one(tailT[:, bass.ds(t, 1), CW - 1:CW - 1 + NB]), win[:, :, CW - 1]))
                        dve.wait_ge(s["silu_done"], l * QKV + t + 1)
                        wc = [prm[:, bass.ds(t + (R_CONV + w * QKV), 1)] for w in range(CW)]
                        step(V.tensor_scalar(conv[:, u], raw[:, u, 0:CONV_N], wc[0], None, ALU.mult))
                        for w in range(1, CW - 1):
                            step(V.scalar_tensor_tensor(conv[:, u], raw[:, u, w:w + CONV_N], wc[w], conv[:, u], ALU.mult, ALU.add))
                        sig(V.scalar_tensor_tensor(conv[:, u], raw[:, u, CW - 1:RAW], wc[CW - 1], conv[:, u], ALU.mult, ALU.add), "conv_done", l * QKV + t + 1)
                    step.leave(QKV // 2)

                def gate_tiles(t0, g0):
                    alone(dve)
                    with dve.Fori(0, H // 2) as i:
                        for u in range(2):
                            tile_done(i * 2 + (t0 + u))
                            moved(V.tensor_tensor(tile_of(gates, i * 2 + (g0 + u)), pj(u), rb[:], ALU.mult), i * 2 + (t0 + u))

                gate_tiles(QKV, 0)
                dve.wait_ge(s["bad_done"], l + 1)
                dve.wait_ge(s["param_loaded"], (l + 1) * 9 * 16)
                step(V.tensor_copy(ga[:, 0:NC, :].rearrange("p c h -> p (c h)"), PS[:, 7, 0:NC * 2 * H]))
                step(V.tensor_copy(ga[:, NC:NG, :].rearrange("p c h -> p (c h)"), PS[:, 6, 64:64 + NB * 2 * H]))
                step(V.tensor_tensor(ga[:, :, H:2 * H], ga[:, :, H:2 * H], adt[:, 0, :].unsqueeze(1).to_broadcast([P, NG, H]), ALU.add))
                sig(V.scalar_tensor_tensor(gs[:], ga[:, :, H:2 * H], -1.0, ga[:, :, H:2 * H], ALU.mult, ALU.max), "gate_pre", l + 1)
                dve.wait_ge(s["rope_loaded"], (l + 1) * 16)
                for r in range(2):
                    step(V.tensor_tensor(rope[:, r], rope[:, r], rb[:], ALU.mult))
                dve.wait_ge(s["gate_exp"], l + 1)
                step(V.tensor_scalar(gb[:], gb[:], 1.0, None, ALU.add))
                step(V.reciprocal(beta[:], gb[:]))
                step(V.scalar_tensor_tensor(gs[:], ga[:, :, H:2 * H], 0.0, gs[:], ALU.max, ALU.add))
                sig(V.scalar_tensor_tensor(g[:], gs[:], -1.0, adt[:, 1, :].unsqueeze(1).to_broadcast([P, NG, H]), ALU.mult, ALU.mult), "g_ready", l + 1)
                h2 = P // 2
                alone(dve)
                with dve.Fori(0, H) as i:
                    step.enter(i, 2 * 4)
                    for u in range(2):
                        j = i * 2 + u
                        t = j + 4 * H
                        tile_done(t)
                        step(V.tensor_tensor(rsw[0:h2, u], PS[h2:P, 2 * u:2 * u + 2, 0:HC], rope[0:h2, 1], ALU.mult))
                        step(V.tensor_tensor(rsw[h2:P, u], PS[0:h2, 2 * u:2 * u + 2, 0:HC], rope[h2:P, 1], ALU.mult))
                        moved(V.tensor_tensor(rcs[:, u], pj(u), rope[:, 0], ALU.mult), t)
                        step(V.tensor_tensor(halves(one(rT[:, bass.ds(j, 1)])), rcs[:, u, :, 0:HALF], rsw[:, u, :, 0:HALF], ALU.add))
                        step(V.tensor_tensor(halves(one(rD[:, bass.ds(j, 1)])), rcs[:, u, :, HALF:HC], rsw[:, u, :, HALF:HC], ALU.add))
                    step.leave(H)
                alone(dve)
                with dve.Fori(0, H // 2) as i:
                    step.enter(i, 2)
                    for u in range(2):
                        j = i * 2 + (u + 2 * H)
                        t = j + 4 * H
                        tile_done(t)
                        step(V.tensor_tensor(halves(one(rT[:, bass.ds(j, 1)])), pj(u)[:, :, 0:HALF], rb[:, :, 0:HALF], ALU.mult))
                        moved(V.tensor_tensor(halves(one(rD[:, bass.ds(j, 1)])), pj(u)[:, :, HALF:HC], rb[:, :, HALF:HC], ALU.mult), t)
                    step.leave(H // 2)
                gate_tiles(7 * H, H)
                dve.wait_ge(s["stat_exp"], l + 1)
                step(V.tensor_tensor(brk[:], beta[:, 0:NC, :], rq[:, :, H:2 * H], ALU.mult))
                step(V.tensor_tensor(c1[:], brk[:], egc[:, 0], ALU.mult))
                step(V.tensor_scalar(rqs[:], rq[:, :, 0:H], SC, None, ALU.mult))
                step(V.tensor_tensor(rqs2[:], rqs[:], rqs[:], ALU.mult))
                step(V.tensor_tensor(gq2[:], cf[:, C_GQ:C_GQ + H], cf[:, C_GQ:C_GQ + H], ALU.mult))
                step(V.tensor_tensor(arkd[:], adec[:].rearrange("p b h -> p h b"), rqd[:, H:2 * H, :], ALU.mult))
                step(V.tensor_tensor(brkd[:], beta[:, NC:NG, :].rearrange("p b h -> p h b"), rqd[:, H:2 * H, :], ALU.mult))

                dve.wait_ge(s["tail_T"], l + 1)
                sig(V.tensor_copy(crow[:], PS[0:CW - 1 + NB, 4:4 + QKV // 4, :].rearrange("p a n -> p (a n)")), "crow_ready", l + 1)
                dve.wait_ge(s["v_T"], l + 1)
                for c in range(NC):
                    ins = V.tensor_tensor(bv[:, c], bank4(c), over_cols(beta[:, c, :]), ALU.mult)
                    if c < NC - 1:
                        step(ins)
                    else:
                        sig(ins, "bv_ready", l + 1)
                def decay_terms(c):
                    if c >= 2:
                        dve.wait_ge(s["decay_mm"], l * NC + (c - 1))
                    sig(V.tensor_tensor(T[:, c % 2], over_heads(m_gt), over_cols(g[:, c, :]), ALU.mult), "decay_in", l * NC + (c + 1))

                for c in range(NC):
                    n = l * NC + c
                    if c == 0:
                        decay_terms(0)
                    if c + 1 < NC:
                        decay_terms(c + 1)
                    dve.wait_ge(s["dk_ready"], n + 1)
                    step(V.tensor_tensor(T[:, 4], T[:, 2 + c % 2], over_heads(m_le), ALU.mult))
                    step(V.tensor_copy(c2[:, c, :], T[:, 4, :, P - 1]))
                    dve.wait_ge(s["chunk_mm"], n + 1)
                    b0 = 4 * (1 - c % 2)
                    step(V.tensor_tensor(MT[:, c], bank4(b0 + 1), T[:, 4], ALU.mult))
                    sig(V.tensor_tensor(PT[:, c], bank4(b0 + 2), T[:, 4], ALU.mult), "chunk_used", n + 1)
                dve.wait_ge(s["inv_init"], (l + 1) * 2)

                def level(m, first=False, last_level=False):
                    def left(c):
                        dve.wait_ge(s["y_mm"], m + (c + 3))
                        sig(V.tensor_tensor(T[:, 2 + c % 2], bank4(c), over_cols(brk[:, c, :]), ALU.mult), "y_ready", m + (c + 1))

                    def right(c):
                        dve.wait_ge(s["x_mm"], m + (c + 1))
                        if not last_level:
                            step(V.tensor_tensor(Xinv[:, c], Xinv[:, c], T[:, 2 + c % 2] if first else bank4(4 + c % 2), ALU.subtract))
                        sig(V.tensor_tensor(XT[:, c], XT[:, c], bank4(6 + c % 2), ALU.subtract), "x_new", m + (c + 5))

                    left(0)
                    for c in range(1, NC):
                        left(c)
                        right(c - 1)
                    right(NC - 1)

                level(l * (LEVELS * NC), first=True)
                alone(dve)
                with dve.Fori(0, LEVELS - 2) as k:
                    step.enter(k, NC)
                    level(l * (LEVELS * NC) + k * NC + NC)
                    step.leave(LEVELS - 2)
                level(l * (LEVELS * NC) + (LEVELS - 1) * NC, last_level=True)

                def norm_sums(i):
                    n, (m, c) = l * 2 * NC + i, divmod(i, NC)
                    dve.wait_ge(s["osq_ready"], n + 1)
                    sig(V.tensor_tensor(nrm[:, 1, :], nrm[:, 0, :], gq2[:] if m else rqs2[:, c, :], ALU.mult), "osum_ready", n + 1)

                def norm_rows(i):
                    n, (m, c) = l * 2 * NC + i, divmod(i, NC)
                    dve.wait_ge(s["orms_ready"], n + 1)
                    step(V.tensor_tensor(nrm[:, 3, :], nrm[:, 2, :], cf[:, C_GQ:C_GQ + H] if m else rqs[:, c, :], ALU.mult))
                    sig(V.tensor_tensor(T[:, 4], T[:, o_at(i)], over_cols(nrm[:, 3, :]), ALU.mult), "on_ready", n + 1)

                dve.wait_ge(s["gates_done"], l + 1)

                def gate_cat(i):
                    n, row = l * 2 * NC + i, (R_GN, R_RN)[i // NC]
                    dve.wait_ge(s["out_T"], n + 1)
                    if i:
                        dve.wait_ge(s["cat_ready"], n)
                    sig(V.scalar_tensor_tensor(T[:, 6], bank4(5), prm[:, row:row + 1], gates[cols_of(i)], ALU.mult, ALU.mult), "catf_ready", n + 1)

                def sample_value(w):
                    n, h = l * 2 * H + w, w % H
                    if w < H:
                        dve.wait_ge(s["dks_mm"], l * H + w + 1)
                        step(V.tensor_tensor(du[:], PS[:, 2, 0:NB], arkd[:, h], ALU.mult))
                        step(V.tensor_tensor(du[:], qkvD[:, 2 * H + h], du[:], ALU.subtract))
                        sig(V.tensor_tensor(du[:], du[:], brkd[:, h], ALU.mult), "dv_ready", n + 1)
                    else:
                        sig(V.tensor_scalar(du[:], rD[:, 2 * H + h], SC, None, ALU.mult), "dv_ready", n + 1)

                def sample_block(w):
                    n = l * 2 * H + w
                    dve.wait_ge(s["dkv_T"], n + 1)
                    step(V.tensor_copy(krow, PS[0:NB, 2, P:3 * P].rearrange("p (a e) -> p a e", a=2)))
                    sig(V.tensor_tensor(vblk, krow[:, 1].unsqueeze(1).to_broadcast([NB, NB, P]), eye_rows.unsqueeze(2).to_broadcast([NB, NB, P]), ALU.mult), "dblk_ready", n + 1)

                def sample_states(w):
                    n, h, st = l * 2 * H + w, w % H, states_of(w)
                    dve.wait_ge(s["dout_mm"], n + 1)
                    dve.wait_ge(s[f"dstate{w % 4}_loaded"], (l * 2 + (w // 4 + 1)) * 16)
                    outer = PS[:, 6:8, :].rearrange("p a (b e) -> p (a b) e", e=P)
                    if w < H:
                        dve.wait_ge(s["ds_decayed"], l * H + w + 1)
                        last = V.tensor_tensor(st, st, outer, ALU.add)
                    else:
                        last = V.scalar_tensor_tensor(st, st, cf[:, C_GS + h:C_GS + h + 1], outer, ALU.mult, ALU.add)
                    sig(last, "dstate_new", n + 1)

                def sample_move(w):
                    n, h = l * 2 * H + w, w % H
                    dve.wait_ge(s["do_mm"], n + 1)
                    o_w = PS[:, 2, 3 * P:3 * P + NB]
                    if w < H:
                        sig(V.scalar_tensor_tensor(oD[:, w], o_w, SC, rqd[:, h], ALU.mult, ALU.mult), "do_moved", n + 1)
                    else:
                        sig(V.tensor_copy(oD[:, w], o_w), "do_moved", n + 1)

                for c in range(NC):
                    n, o_rows = l * NC + c, T[:, o_at(c)]
                    dve.wait_ge(s["ks_mm"], n + 1)
                    step(V.tensor_tensor(T[:, 0], bank4(0), over_cols(c1[:, c, :]), ALU.mult))
                    sig(V.tensor_tensor(T[:, 0], bv[:, c], T[:, 0], ALU.subtract), "r_ready", n + 1)
                    dve.wait_ge(s["qs_mm"], n + 1)
                    step(V.tensor_tensor(o_rows, bank4(1), over_cols(egc[:, 0, c, :]), ALU.mult))
                    if c:
                        sample_move(c - 1)
                    if c:
                        norm_rows(c - 1)
                    dve.wait_ge(s["vn_mm"], n + 1)
                    step(V.tensor_copy(T[:, 1], bank4(0)))
                    sig(V.tensor_tensor(T[:, 2], T[:, 1], over_cols(c2[:, c, :]), ALU.mult), "vs_ready", n + 1)
                    sample_value(c)
                    if c:
                        gate_cat(c - 1)
                    sample_block(c)
                    dve.wait_ge(s["od_mm"], n + 1)
                    dve.wait_ge(s["s_decayed"], n + 1)
                    sig(V.tensor_tensor(S[:], S[:], bank4(4), ALU.add), "s_ready", l * (NC + 1) + c + 2)
                    sig(V.tensor_tensor(o_rows, o_rows, bank4(3), ALU.add), "o_ready", l * 2 * NC + c + 1)
                    sample_states(c)
                    norm_sums(c)
                for c in range(NC):
                    n, i = l * NC + c, NC + c
                    sample_value(i)
                    sample_move(i - 1)
                    dve.wait_ge(s["rtr_mm"], n + 1)
                    step(V.tensor_tensor(T[:, 1], bank4(1), over_cols(cf[:, C_GV:C_GV + H]), ALU.mult))
                    sig(V.tensor_tensor(T[:, 2], bank4(3), over_heads(m_le), ALU.mult), "rv_ready", n + 1)
                    norm_rows(i - 1)
                    sample_block(i)
                    dve.wait_ge(s["rod_mm"], n + 1)
                    step(V.tensor_tensor(Sr[:], Sr[:], bank4(0), ALU.add))
                    sig(V.tensor_tensor(Sr[:], Sr[:], over_cols(cf[:, C_GC:C_GC + H]), ALU.mult), "rs_ready", l * (NC + 1) + c + 2)
                    sig(V.tensor_copy(T[:, o_at(i)], bank4(4)), "o_ready", l * 2 * NC + i + 1)
                    gate_cat(i - 1)
                    sample_states(i)
                    norm_sums(i)
                sample_move(2 * NC - 1)
                sig(V.tensor_tensor(dn[:], oD[:], oD[:], ALU.mult), "dsq_ready", l + 1)
                norm_rows(2 * NC - 1)
                dve.wait_ge(s["drms_ready"], l + 1)
                dve.wait_ge(s["gates_done"], l + 1)
                step(V.tensor_tensor(oD[:], oD[:], drm[:], ALU.mult))
                for m, r in enumerate((R_GN, R_RN)):
                    hs = slice(m * H, (m + 1) * H)
                    ins = V.scalar_tensor_tensor(catD[:, hs].rearrange("p h (a b) -> p (h a) b", a=2), oD[:, hs].rearrange("p h (a b) -> p (h a) b", a=2), prm[:, r:r + 1],
                                               gates[:, hs].rearrange("p h a n -> p (h a) n")[:, :, HALF:HC], ALU.mult, ALU.mult)
                    if m == 0:
                        step(ins)
                    else:
                        sig(ins, "catD_ready", l + 1)
                gate_cat(2 * NC - 1)
                dve.wait_ge(s["dcath_ready"], l + 1)
                dec = Xl[:].rearrange("p k a n -> p (k a) n")[:, :, HALF:HC]
                dech = Xh[:].rearrange("p k a n -> p (k a) n")[:, :, HALF:HC].bitcast(fp32)
                sig(V.tensor_tensor(dec, catD[:].rearrange("p h (a b) -> p (h a) b", a=2), dech, ALU.subtract), "dcat_ready", l + 1)

                def branch(n, t0, s0, per, dst, row, h0, then=None):
                    dve.wait_ge(s["norm_sum"], l * 2 + (n // 2 + 1))
                    step(V.memset(ss[:], 0.0))
                    alone(dve)
                    with dve.Fori(0, KT // 2) as i:
                        for u in range(2):
                            k = i * 2 + u
                            dve.wait_ge(s["slab_done"], l * SLABS + k * per + (s0 + per + NW))
                            moved(V.tensor_copy(tile_of(dst, k), pj(u)), k + t0)
                            add_squares(n, k, u)
                    dve.wait_ge(s["rb_ready"], l * 4 + n + 2)
                    for k in range(KT):
                        step(V.scalar_tensor_tensor(upd[:], dst[:, k], prm[:, row + k:row + k + 1], rb[:], ALU.mult, ALU.mult))
                        sig(V.tensor_tensor(hT[:, k], hT[:, k], upd[:], ALU.add), "h_ready", h0 + k + 1)
                        if then and k:
                            then(k - 1)
                    if then:
                        then(KT - 1)

                for w in range(4):
                    dve.wait_ge(s[f"dstate{w}_stored"], (l + 1) * 2 * 16)
                branch(1, T_OUT, S_OUT, 1, mT, R_MPOST, l * 2 * KT + KT, then=lambda k: rest_x(2, k, R_FPRE))
                dve.wait_ge(s["rb_ready"], l * 4 + 4)
                alone(dve)
                with dve.Fori(0, FT // 2) as i:
                    for u in range(2):
                        j = i * 2 + u
                        dve.wait_ge(s["slab_done"], l * SLABS + j * 2 + (S_GU + 1 + NW))
                        moved(V.tensor_tensor(gp[:, u], pj(0), rb[:], ALU.mult), j * 2 + T_GU)
                        dve.wait_ge(s["slab_done"], l * SLABS + j * 2 + (S_GU + 2 + NW))
                        moved(V.tensor_tensor(up[:], pj(1), rb[:], ALU.mult), j * 2 + (T_GU + 1))
                        dve.wait_ge(s["gate_silu"], l * FT + j + 1)
                        sig(V.tensor_tensor(ab[:, u], gp[:, u], up[:], ALU.mult), "a_ready", l * FT + j + 1)
                        dve.wait_ge(s["ah_ready"], l * FT + j + 1)
                        sig(V.tensor_tensor(tile_of(actL, j), ab[:, u], tile_of(actH, j).bitcast(fp32), ALU.subtract), "act_ready", l * FT + j + 1)
                branch(3, T_DN, S_DN, len(PIECES), fT, R_FPOST, l * 2 * KT + 2 * KT)
                step.leave(DEPTH)

            step(V.tensor_copy(hd[:, :, 0:NBH], hT[:, :, 0, HALF:HC]))
            sig(V.tensor_copy(hd[:, :, NBH:NB], hT[:, :, 1, HALF:HC]), "hd_ready", 1)
            for c in range(NC):
                dve.wait_ge(s["y_T"], c + 1)
                b = 2 * (c % 2)
                sig(V.tensor_copy(ytok[:, c, :].rearrange("p (a n) -> p a n", a=2), PS[:, b:b + 2, :]), "y_moved", c + 1)
            dve.wait_ge(s["y_T"], NC + 1)
            sig(V.tensor_copy(yd[:].rearrange("p (a n) -> p a n", a=2), PS[0:NB, 4:6, :]), "y_moved", NC + 1)


_INS = ["x_prompt", "x_sample", "state_conv", "state_gdn", "state_ret", "w_in", "conv_w", "a_log", "dt_bias",
        "gdn_norm_w", "ret_norm_w", "w_out", "norm_mix_pre", "norm_mix_post", "norm_ffn_pre", "norm_ffn_post",
        "w_gate_up", "w_down"]


def _constants(seq, nb, heads, past_len=4096, rope_base=10000.0):
    P = 128
    i = np.arange(P)
    gamma = 1.0 - 2.0 ** (-5.0 - np.arange(heads))
    cols = [np.eye(P), np.ones((P, P)), (i[:, None] <= i[None, :]), (i[:, None] > i[None, :]),
            gamma[None, :] ** (i[:, None] + 1.0), gamma[None, :] ** -(i[:, None] + 1.0) * P ** -0.5,
            np.broadcast_to(gamma[None, :] ** P, (P, heads)), np.broadcast_to(gamma[None, :], (P, heads))]
    c_f32 = np.concatenate([np.asarray(c, np.float64) for c in cols], 1).astype(np.float32)
    half = P // 2
    inv = np.float32(rope_base) ** (-np.arange(half, dtype=np.float32) / np.float32(half))
    at = np.arange(seq, dtype=np.float32)
    new = np.full(nb // 2, past_len, np.float32)
    pos = np.concatenate([at[:seq // 2], new, at[seq // 2:], new])
    ang = (pos[None, :] * inv[:, None]).astype(np.float32).astype(np.float64)
    cos, sin = np.cos(ang), np.sin(ang)
    rope = np.stack([np.concatenate([cos, cos]), np.concatenate([-sin, sin])], 1).astype(np.float32)
    rope = rope.reshape(P, 2, 2, -1)
    mask = np.zeros((P, 7, P))
    for k in range(7):
        j, r = i[:, None], i[None, :]
        mask[:, k, :] = (j >> (k + 1) == r >> (k + 1)) & ((r >> k) & 1 == 1) & ((j >> k) & 1 == 0)
    return c_f32, rope, mask


def kernel(**inputs):
    import concourse.bacc as bacc
    import ml_dtypes
    from concourse.bass_utils import run_bass_kernel_spmd

    nc = bacc.Bacc("TRN2", target_bir_lowering=False, num_devices=1)
    arrays, args = {}, []

    def add(name, a):
        arrays[name] = a
        args.append(nc.dram_tensor(name, a.shape, mybir.dt.from_np(a.dtype), kind="ExternalInput").ap())

    for name in _INS:
        add(f"in_{name}", np.ascontiguousarray(inputs[name]))
    depth, nb, heads, dim, _ = inputs["state_gdn"].shape
    _, seq, d = inputs["x_prompt"].shape
    cw = inputs["conv_w"].shape[1]
    c_f32, rope, mask = _constants(seq, nb, heads)
    add("c_f32", c_f32)
    add("c_rope", rope)
    add("c_mask", mask.astype(ml_dtypes.bfloat16))
    width = 3 * heads * dim
    outs = [(1, seq, d), (nb, 1, d), (depth, 1, cw - 1, width), (depth, 1, heads, dim, dim),
            (depth, 1, heads, dim, dim), (depth, nb, cw - 1, width), (depth, nb, heads, dim, dim),
            (depth, nb, heads, dim, dim)]
    for i, shape in enumerate(outs):
        args.append(nc.dram_tensor(f"out_{i}", shape, mybir.dt.float32, kind="ExternalOutput").ap())
    trunk(nc, *args)
    r = run_bass_kernel_spmd(nc, [arrays], core_ids=[0])
    return tuple(r.results[0][f"out_{i}"] for i in range(len(outs)))
```
